# Optimizing a Trainium2 kernel written in Bass

```python
import jax, jax.numpy as jnp
from jax import lax
import numpy as np

D_MODEL = 2048
BATCH = 1
SEQ = 1024
DEPTH = 1
DEC_BATCH = 8
DEC_SEQ = 16
PAST_LEN = 512

CHUNK = 64
QBLOCK = 128
D_ATTN = D_MODEL // 2
D_CONV = D_MODEL - D_ATTN
N_HEADS = 8
HEAD_DIM = D_ATTN // N_HEADS
N_KV_HEADS = 2
KV_GROUP = N_HEADS // N_KV_HEADS
KV_DIM = N_KV_HEADS * HEAD_DIM
N_IDX_HEADS = 16
IDX_DIM = 64
TOPK_MAX = 256
CONV_WIDTH = 3
RMS_EPS = 1e-6
SPLIT_SIZES = (D_ATTN, KV_DIM, KV_DIM, D_ATTN, N_IDX_HEADS * IDX_DIM, IDX_DIM, N_IDX_HEADS,
               D_CONV, D_CONV, D_CONV, D_CONV)
D_PROJ = 3 * D_ATTN + 2 * KV_DIM + N_IDX_HEADS * IDX_DIM + IDX_DIM + N_IDX_HEADS + D_CONV * 3

kernel_name = "hybrid_dsa_shortconv_stream_step"

def _offsets():
    offs, acc = [], 0
    for s in SPLIT_SIZES[:-1]:
        acc += s
        offs.append(acc)
    return offs

def _rmsnorm(x, g):
    xf = x.astype(jnp.float32)
    xf = xf * lax.rsqrt(jnp.mean(xf * xf, axis=-1, keepdims=True) + RMS_EPS)
    return (xf * g.astype(jnp.float32)).astype(x.dtype)

def _project(x, g_pre, w_in):
    b, t, _ = x.shape
    h = _rmsnorm(x, g_pre)
    z = jnp.einsum('btd,de->bte', h, w_in)
    q, k, v, ga, qi, ki, wi, bg, cg, hc, gb = jnp.split(z, _offsets(), axis=-1)
    q = q.reshape(b, t, N_KV_HEADS, KV_GROUP, HEAD_DIM)
    k = k.reshape(b, t, N_KV_HEADS, HEAD_DIM)
    v = v.reshape(b, t, N_KV_HEADS, HEAD_DIM)
    qi = qi.reshape(b, t, N_IDX_HEADS, IDX_DIM)
    return q, k, v, ga, qi, ki, wi, bg, cg, hc, gb

def _sparse_attend(q, qi, wi, qpos, k_all, v_all, ki_all, topk):
    b, tq = q.shape[:2]
    s = k_all.shape[1]
    qchunk = qpos // CHUNK
    kchunk = jnp.arange(s, dtype=jnp.int32) // CHUNK
    iscore = jnp.einsum('bthd,bsd->btsh', qi, ki_all, preferred_element_type=jnp.float32) * (IDX_DIM ** -0.5)
    iscore = jnp.einsum('btsh,bth->bts', jax.nn.relu(iscore), wi.astype(jnp.float32)) * (N_IDX_HEADS ** -0.5)
    admissible = kchunk[None, :] <= qchunk[:, None]
    iscore = jnp.where(admissible[None], iscore, -jnp.inf)
    _, sel = lax.top_k(iscore, topk)
    gather = jax.vmap(lambda rows, idx: rows[idx])
    k_sel = gather(k_all, sel)
    v_sel = gather(v_all, sel)
    logits = jnp.einsum('btkgd,btnkd->btkgn', q, k_sel, preferred_element_type=jnp.float32) * (HEAD_DIM ** -0.5)
    valid = (sel // CHUNK) <= qchunk[None, :, None]
    logits = jnp.where(valid[:, :, None, None, :], logits, -jnp.inf)
    probs = jax.nn.softmax(logits, axis=-1).astype(v_all.dtype)
    out = jnp.einsum('btkgn,btnkd->btkgd', probs, v_sel)
    return out.reshape(b, tq, D_ATTN)

def _prompt_attention(q, qi, wi, k, v, ki):
    b, t = q.shape[:2]
    nblk = t // QBLOCK
    topk = min(TOPK_MAX, t // 4)

    def to_blocks(a):
        return jnp.moveaxis(a.reshape((b, nblk, QBLOCK) + a.shape[2:]), 1, 0)

    qpos = jnp.arange(t, dtype=jnp.int32).reshape(nblk, QBLOCK)

    def block(args):
        qb, qib, wib, pb = args
        return _sparse_attend(qb, qib, wib, pb, k, v, ki, topk)

    out = lax.map(block, (to_blocks(q), to_blocks(qi), to_blocks(wi), qpos))
    return jnp.moveaxis(out, 0, 1).reshape(b, t, D_ATTN)

def _short_conv(bg, cg, hc, prev, w_conv):
    t = hc.shape[1]
    u = cg * hc
    u_pad = jnp.concatenate([prev.astype(u.dtype), u], axis=1)
    conv = w_conv[0] * u_pad[:, 0:t]
    for j in range(1, CONV_WIDTH):
        conv = conv + w_conv[j] * u_pad[:, j:j + t]
    return bg * conv, u_pad[:, -(CONV_WIDTH - 1):]

def _merge(x, attn, ga, conv, gb, w_out, g_post):
    z = jnp.concatenate([attn * jax.nn.silu(ga), conv * jax.nn.silu(gb)], axis=-1)
    return x + _rmsnorm(jnp.einsum('bte,ed->btd', z, w_out), g_post)

def _prompt_layer(x, g_pre, w_in, w_conv, w_out, g_post):
    q, k, v, ga, qi, ki, wi, bg, cg, hc, gb = _project(x, g_pre, w_in)
    attn = _prompt_attention(q, qi, wi, k, v, ki)
    zeros = jnp.zeros((x.shape[0], CONV_WIDTH - 1, D_CONV), x.dtype)
    conv, conv_state = _short_conv(bg, cg, hc, zeros, w_conv)
    y = _merge(x, attn, ga, conv, gb, w_out, g_post)
    return y, k, v, ki, conv_state

def _sample_layer(x, past_k, past_v, past_ik, prev_conv, g_pre, w_in, w_conv, w_out, g_post):
    q, k, v, ga, qi, ki, wi, bg, cg, hc, gb = _project(x, g_pre, w_in)
    past = past_k.shape[1]
    ts = x.shape[1]
    k_all = jnp.concatenate([past_k.astype(k.dtype), k], axis=1)
    v_all = jnp.concatenate([past_v.astype(v.dtype), v], axis=1)
    ik_all = jnp.concatenate([past_ik.astype(ki.dtype), ki], axis=1)
    qpos = past + jnp.arange(ts, dtype=jnp.int32)
    topk = min(TOPK_MAX, (past + ts) // 4)
    attn = _sparse_attend(q, qi, wi, qpos, k_all, v_all, ik_all, topk)
    conv, conv_state = _short_conv(bg, cg, hc, prev_conv, w_conv)
    y = _merge(x, attn, ga, conv, gb, w_out, g_post)
    return y, k, v, ki, conv_state

def setup_inputs(seed: int = 0) -> dict:
    key = jax.random.key(seed)
    ks = jax.random.split(key, 12)
    f32 = jnp.float32
    return {
        "x_prompt": jax.random.normal(ks[0], (BATCH, SEQ, D_MODEL), f32),
        "x_sample": jax.random.normal(ks[1], (DEC_BATCH, DEC_SEQ, D_MODEL), f32),
        "cache_k": jax.random.normal(ks[2], (DEPTH, DEC_BATCH, PAST_LEN, N_KV_HEADS, HEAD_DIM), f32),
        "cache_v": jax.random.normal(ks[3], (DEPTH, DEC_BATCH, PAST_LEN, N_KV_HEADS, HEAD_DIM), f32),
        "cache_idx_k": jax.random.normal(ks[4], (DEPTH, DEC_BATCH, PAST_LEN, IDX_DIM), f32),
        "state_conv": jax.random.normal(ks[5], (DEPTH, DEC_BATCH, CONV_WIDTH - 1, D_CONV), f32),
        "g_pre": 1.0 + 0.05 * jax.random.normal(ks[6], (DEPTH, D_MODEL), f32),
        "w_in": jax.random.normal(ks[7], (DEPTH, D_MODEL, D_PROJ), f32) * D_MODEL ** -0.5,
        "w_conv": jax.random.normal(ks[8], (DEPTH, CONV_WIDTH, D_CONV), f32) * CONV_WIDTH ** -0.5,
        "w_out": jax.random.normal(ks[9], (DEPTH, D_MODEL, D_MODEL), f32) * D_MODEL ** -0.5,
        "g_post": 1.0 + 0.05 * jax.random.normal(ks[10], (DEPTH, D_MODEL), f32),
    }

def reference(x_prompt, x_sample, cache_k, cache_v, cache_idx_k, state_conv, g_pre, w_in, w_conv, w_out, g_post):
    xp, xs = x_prompt, x_sample
    kp_l, vp_l, ikp_l, cp_l = [], [], [], []
    ks_l, vs_l, iks_l, cs_l = [], [], [], []
    for l in range(DEPTH):
        xp, kp, vp, ikp, cp = _prompt_layer(xp, g_pre[l], w_in[l], w_conv[l], w_out[l], g_post[l])
        xs, ksm, vsm, iks, csm = _sample_layer(xs, cache_k[l], cache_v[l], cache_idx_k[l], state_conv[l],
                                               g_pre[l], w_in[l], w_conv[l], w_out[l], g_post[l])
        kp_l.append(kp); vp_l.append(vp); ikp_l.append(ikp); cp_l.append(cp)
        ks_l.append(ksm); vs_l.append(vsm); iks_l.append(iks); cs_l.append(csm)
    new_k_prompt = jnp.stack(kp_l)
    new_v_prompt = jnp.stack(vp_l)
    new_ik_prompt = jnp.stack(ikp_l)
    conv_prompt = jnp.stack(cp_l)
    new_k_sample = jnp.stack(ks_l)
    new_v_sample = jnp.stack(vs_l)
    new_ik_sample = jnp.stack(iks_l)
    conv_sample = jnp.stack(cs_l)
    return (xp, xs, new_k_prompt, new_v_prompt, new_ik_prompt, conv_prompt,
            new_k_sample, new_v_sample, new_ik_sample, conv_sample)


_drawn_inputs = setup_inputs


def setup_inputs(seed=0):
    import zlib

    import numpy as np

    out = dict(_drawn_inputs(seed))
    spreads = {}
    factors = {}
    for name, (base, spread) in spreads.items():
        noise = np.random.default_rng([zlib.crc32(name.encode()), seed]).standard_normal(out[name].shape)
        drawn = base * np.exp(spread * noise) if base else spread * noise
        out[name] = __import__('jax').numpy.asarray(drawn.astype(out[name].dtype))
    for name, factor in factors.items():
        out[name] = (out[name] * factor).astype(out[name].dtype)
    return out
```

```python
from contextlib import ExitStack

import concourse.bass as bass
from concourse import mybir

F32 = mybir.dt.float32
F32R = mybir.dt.float32r
BF16 = mybir.dt.bfloat16
ALU = mybir.AluOpType
ACT = mybir.ActivationFunctionType
AX_X = mybir.AxisListType.X

P = 128
D = 2048
KT = D // P
SEQ, NB, NS = 1024, 8, 16
PAST = 512
T_A, T_B = 512 + NB * NS, 512
T_ALL = T_A + T_B
TOKENS = {"A": T_A, "B": T_B}
COLUMN = {"A": 0, "B": T_A}
TT = {"A": T_A // P, "B": T_B // P}
HD, IH, ID = 128, 16, 64
TOPK = 256
KEYS_S = PAST + NS
HALF_S = KEYS_S // 2
TOPK_S = min(TOPK, KEYS_S // 4)
PAD_S = -TOPK_S % 8
ROUNDS, ROUNDS_S = TOPK // 8, (TOPK_S + PAD_S) // 8
SCALE = HD ** -0.5
EPS = 1e-6
NEG_MASK = -1e30
NEG_LATER = -3.0e38
NEG_TAKEN = -3.4e38
NEG_CUT = -3.3e38

Q0, K0, V0, GA0, QI0, KI0 = 0, 1024, 1280, 1536, 2560, 3584
BG0, CG0, HC0, GB0 = 3664, 4688, 5712, 6736

_FIRST = ([("kiwi", 0, KI0)] + [("k", i, K0 + P * i) for i in range(2)] + [("v", i, V0 + P * i) for i in range(2)]
          + [("qi", i, QI0 + P * i) for i in range(8)] + [("q", i, Q0 + P * i) for i in range(8)])
_CONV = [t for c in range(8) for t in (("cg", c, CG0 + P * c), ("hc", c, HC0 + P * c),
                                       ("bg", c, BG0 + P * c), ("gb", c, GB0 + P * c))]
_GATE = [("ga", i, GA0 + P * i) for i in range(8)]
PROJ = {"A": _FIRST + _CONV + _GATE, "B": _FIRST + _GATE[:6] + _CONV + _GATE[6:]}
OUTP = [("o", i, P * i) for i in range(KT)]
NP, NO = len(PROJ["A"]), len(OUTP)
TILES = ([("A", *t) for t in PROJ["A"]] + [("B", *t) for t in PROJ["B"]]
         + [("A", *t) for t in OUTP] + [("B", *t) for t in OUTP])
NT = len(TILES)
OUT_A, OUT_B = 2 * NP, 2 * NP + NO
PHASE_START = (0, NP, OUT_A, OUT_B)
PHASE_LAST = (NP - 1, OUT_A - 1, OUT_B - 1, NT - 1)
SLOTS = 8
PER = KT // SLOTS
RING = 3
TURNED = ("kiwi", "k", "v", "o")
SPILLED = ("kiwi", "k", "qi", "q", "ga", "gb")
BUFFERED = SPILLED + ("v", "o")


def tile_number(group, kind, index):
    return next(n for n, t in enumerate(TILES) if t[:3] == (group, kind, index))


EV = {}
EV_SPILLS = {}
TURN = {}
_c = [0, 0]
for _i, _t in enumerate(TILES):
    if _t[1] in BUFFERED:
        EV[_i] = len(EV)
        _c[EV[_i] % 2] += _t[1] in SPILLED
        EV_SPILLS[_i] = tuple(_c)
    if _t[1] in TURNED:
        TURN[_i] = len(TURN)
EV_TILE = {v: k for k, v in EV.items()}


def turned_before(n, group=None, kinds=TURNED):
    return sum(1 for x in TURN if x < n and TILES[x][1] in kinds and group in (None, TILES[x][0]))


def block_column(b):
    return P * b + (P if b >= 4 else 0)


def group_of(b):
    return "A" if b < 4 else "B"


def pieces(b):
    n = P * (b + 1)
    k = 1 if n <= 512 else 2
    return k, n // k


US_A, US_B = 1.63, 1.30


TKF, FA, FB, FS = 1.1, 1.0, 1.2, 1.0


def index_steps(b, us):
    n = P * (b + 1)
    out = [(("QI", b, 0), 1)]
    for hp in range(IH // 2):
        out += [(("HEAD", b, hp), (2 * (n + 60) / 960 * 1.15 + 0.3) / us)] + ([(("QI", b, 1), 0)] if hp == 2 else [])
    out[-1] = (out[-1][0], out[-1][1] + 2 / us)
    return out + [(("TK", b, r), TKF * 2 * 2 * (n + 190) / 960 / us) for r in range(0, ROUNDS, 2)]


def stream_index_steps():
    out = [(("QS",), 2)]
    for b in range(NB):
        out += [(("IKS", b), 2), (("HS", b, 0), 2), (("SEL", b, 0), 0), (("HS", b, 1), 2), (("SEL", b, 1), 0)]
    return out + [(("ISCS",), 1)] + [(("TK", "s", r), 2) for r in range(0, ROUNDS_S, 2)]


def softmax_steps(group, us):
    out = []
    blocks = range(4) if group == "A" else range(4, 8)
    units = [(b, kv) for kv in range(2) for b in blocks]
    for i, (b, kv) in enumerate(units):
        if i == 0:
            out += [(("KK", group, 0), 2), (("QQ", *units[0]), 2)]
        if b == blocks[0]:
            out += [(("VV", group, kv), 1)]
        n = P * (b + 1)
        out += [(("S", b, kv, h), ((n + 60) / 960 + n / 1920 + 0.6) / us) for h in range(4)]
        if i + 1 < len(units):
            if b == blocks[-1]:
                out += [(("KK", group, 1), 0)]
            out += [(("QQ", *units[i + 1]), 0)]
        out += [(("NRM", b, kv), (1 + n / 1000) / us)]
        out += [(("PT", b, kv, j), 1.4 / us) for j in range(b + 1)]
        out += [(("ZZ", b, kv), 1.5 / us)]
    return out


def stream_softmax_steps():
    out = [(("QQS",), 1), (("KS", 0), 3)]
    for b in range(NB):
        out += [(("SS", b), 2)] + ([(("KS", b + 1), 2)] if b + 1 < NB else []) + [(("PS", b), 1.5), (("VS", b), 1)]
    return out + [(("ZS",), 1)]


PLACED = [0]


def timetable():
    side = {}

    def place(steps, tile, end):
        at = float(SLOTS * tile)
        at = max(at, float(PLACED[0]))
        for step, width in steps:
            side.setdefault(min(int(at), SLOTS * end - 1), []).append(step)
            at += width
        PLACED[0] = at

    place([(("CHUNKS", 0), 1), (("CHUNKS", 1), 1), (("IK", "A"), 2)]
          + index_steps(2, US_A) + index_steps(3, US_A) + stream_index_steps(), 22, NP - 7)
    place([(("NX", i), 8) for i in range(5, 9)], NP - 6, NP - 1)
    softmax_b = softmax_steps("B", US_A)
    cut = [s[0] for s in softmax_b].index(("ZZ", 7, 0)) + 1
    early = [s for s in softmax_b[:cut] if s[0] not in (("KK", "B", 1), ("QQ", 4, 1))]
    place([(s, FA * w) for s, w in softmax_steps("A", US_B)] + [(s, FS * w) for s, w in stream_softmax_steps()], NP + 1.5, NP + 22)
    place([(("IK", "B"), 3)] + [s for b in range(4, 8) for s in index_steps(b, US_B)] + [(s, w * FB) for s, w in early], NP + 17, 2 * NP+2)
    place([(("KK", "B", 1), 2), (("QQ", 4, 1), 2)] + [(s, w * FB) for s, w in softmax_b[cut:]], 2 * NP + 1.7, OUT_B - 1)
    place([(("RMS", "A"), 3)] + [(("FIN", i), 16) for i in range(5)], OUT_B + 1, OUT_B + 14)
    side[TAIL] = [("RMS", "B")] + [("FIN", i) for i in range(5, 9)]
    return side


TAIL = SLOTS * NT
SIDE = timetable()
ORDER = [s for slot in sorted(SIDE) for s in SIDE[slot]]
NTH = {}
for _s in ORDER:
    NTH[_s] = sum(1 for x in NTH if x[0] == _s[0])
POSITION = {s: i for i, s in enumerate(ORDER)}


def before(step, kind):
    return sum(1 for s in ORDER[:POSITION[step]] if s[0] == kind)


AHEAD = 10
SLOT_OF = {s: slot for slot in SIDE for s in SIDE[slot]}
LOADING = ("IK", "QI", "QS", "IKS", "KK", "VV", "QQ", "QQS", "KS", "SS", "NX", "FIN")


def released_by(step):
    kind, n = step[0], NTH[step]
    same = [s for s in ORDER if s[0] == kind]
    before_it = ORDER[:POSITION[step]]
    if kind in ("KS", "QI") and n > 0:
        return same[n - 1]
    if kind == "KK" and n > 0:
        return [s for s in ORDER if s[0] == "VV"][n - 1]
    if kind == "VV":
        return [s for s in ORDER if s[0] == "KK"][n]
    if kind == "QQ":
        return max([s for s in before_it if s[0] == "TK"][-1:] + [s for s in ORDER if s[0] == "ZZ"][max(n - 2, 0):max(n - 1, 0)],
                   key=POSITION.get)
    if kind in ("IKS", "FIN") and n > 1:
        return same[n - 2]
    if kind == "SS":
        return [s for s in before_it if s[0] in ("VS", "ZZ")][-1]
    if kind == "QQS":
        return [s for s in before_it if s[0] in ("QQ", "VV")][-1]
    if step == ("IK", "B"):
        return ("ZS",)
    return None


def spilled_at(step):
    kind = step[0]
    source = {"IK": ("kiwi", 0), "QI": ("qi", 7), "QS": ("qi", 7), "KK": ("k", 1), "VV": ("v", 1), "QQ": ("ga", 3 + 4 * (step[-1] == 1)),
              "QQS": ("ga", 7), "FIN": ("o", KT - 1)}.get(kind)
    if source is None:
        return 0
    group = step[1] if kind in ("IK", "KK", "VV") else group_of(step[1]) if kind in ("QI", "QQ") else "A"
    return SLOTS * (tile_number(group, *source) + 1) + 5


LOADS = {}
for _s in ORDER:
    if _s[0] in LOADING and SLOT_OF[_s] < TAIL:
        _free = released_by(_s)
        LOADS.setdefault(max(SLOT_OF[_s] - AHEAD, SLOT_OF[_free] + (_free[0] in ("TK", "ZS")) if _free else 0, spilled_at(_s)),
                         []).append(_s)


def last_rounds(step):
    return step[2] + 2 >= (ROUNDS_S if step[1] == "s" else ROUNDS)


MASKS = [s[1] for s in ORDER if s[0] == "CHUNKS" or (s[0] == "TK" and last_rounds(s))]
MASKS_A = sum(1 for b in MASKS if b == "s" or b < 4)
UNITS_A = sum(1 for s in ORDER if s[0] == "ZZ" and s[1] < 4)
UNITS = sum(1 for s in ORDER if s[0] == "ZZ")
HEADS_A = 2 * sum(1 for s in ORDER if s[0] == "HEAD" and s[1] < 4)
HEADS = 2 * sum(1 for s in ORDER if s[0] == "HEAD")
QI_A = sum(1 for s in ORDER if s[0] == "QI" and s[1] < 4)
QI_ALL = sum(1 for s in ORDER if s[0] == "QI")
PT_A = sum(1 for s in ORDER if s[0] == "PT" and s[1] < 4)

UNITS_X = [(i, j) for i in range(5) for j in range(4)] + [(5 + i, j) for j in range(4) for i in range(4)]
NX_A, NX_B = 20, 16


def build(nc, x_prompt, x_sample, cache_k, cache_v, cache_idx_k, state_conv, g_pre, w_in, w_conv, w_out, g_post,
          y_prompt, y_sample, new_k_p, new_v_p, new_ik_p, conv_p, new_k_s, new_v_s, new_ik_s, conv_s):
    def scratch(name, rows, cols=T_ALL, dt=F32):
        return nc.dram_tensor(name, (rows, cols), dt).ap()

    z_q, z_k, z_kiwi, z_qi = scratch("z_q", 1024), scratch("z_k", 256), scratch("z_kiwi", P), scratch("z_qi", 1024)
    z_ga, z_mix = scratch("z_ga", 1024), scratch("z_mix", D)
    z_mask = scratch("z_mask", 9 * P, SEQ, BF16)
    z_og = scratch("z_og", T_A, D)
    spill_to = {"q": z_q, "k": z_k, "kiwi": z_kiwi, "qi": z_qi, "ga": z_ga, "gb": z_mix[1024:D]}

    w_in_v = w_in[0].rearrange("(k p) e -> p k e", p=P)
    w_out_v = w_out[0].rearrange("(k p) e -> p k e", p=P)
    xs = x_sample.rearrange("b t d -> (b t) d")
    ys = y_sample.rearrange("b t d -> (b t) d")

    def token_rows(prompt, streams, i):
        if i == 4:
            return streams
        r = P * (i if i < 4 else i - 1)
        return prompt[r:r + P]

    with ExitStack() as ctx:
        def semaphores(names):
            return tuple(ctx.enter_context(nc.semaphore(name)) for name in names.split())

        def semaphore_ring(name, k):
            return [ctx.enter_context(nc.semaphore(f"{name}{i}")) for i in range(k)]

        (sem_w_hi, sem_w_lo, sem_gemm, sem_passed, sem_nat_pe, sem_nat_cp, sem_nat_sq, sem_cg_rdy, sem_hc_rdy,
         sem_gb_silu, sem_gb_used, sem_const, sem_wcv_ld, sem_st_ld, sem_g_ld) = semaphores(
            "w_hi w_lo gemm passed nat_pe nat_cp nat_sq cg_rdy hc_rdy gb_silu gb_used const wcv_ld st_ld g_ld")
        (sem_x_ssq, sem_x_ms, sem_x_rt, sem_x_rdy, sem_x_read, sem_x_tr, sem_x_hi, sem_x_lo, sem_cs_out, sem_z_hi,
         sem_z_lo) = semaphores(
            "x_ssq x_ms x_rt x_rdy x_read x_tr x_hi x_lo cs_out z_hi z_lo")
        (sem_ik_ld, sem_ik_hi, sem_ik_lo, sem_qi_ld, sem_qi_hi, sem_qi_lo, sem_head_pe, sem_relu, sem_isum, sem_mask,
         sem_mask_out) = semaphores(
            "ik_ld ik_hi ik_lo qi_ld qi_hi qi_lo head_pe relu isum mask mask_out")
        (sem_qs_ld, sem_iks_tr, sem_iks_cp, sem_hs_pe, sem_hs_r, sem_sel_pe, sem_iscs) = semaphores(
            "qs_ld iks_tr iks_cp hs_pe hs_r sel_pe iscs")
        (sem_kk_ld, sem_kk_hi, sem_kk_lo, sem_vv_ld, sem_vv_hi, sem_vv_lo, sem_qq_hi, sem_qq_lo, sem_s_pe, sem_s_max,
         sem_s_nb, sem_s_exp, sem_s_norm, sem_pt_pe, sem_pt_hi, sem_pt_lo, sem_pv_pe, sem_z_dve) = semaphores(
            "kk_ld kk_hi kk_lo vv_ld vv_hi vv_lo qq_hi qq_lo s_pe s_max s_nb s_exp s_norm pt_pe pt_hi pt_lo pv_pe "
            "z_dve")
        (sem_z_out, sem_qqs_ld, sem_ks_tr, sem_ks_cp, sem_ss_pe, sem_ss_max, sem_ss_nb, sem_ss_exp, sem_ss_norm,
         sem_ps_tr, sem_ps_cp, sem_pvs_pe, sem_vs_dve, sem_zs_out) = semaphores(
            "z_out qqs_ld ks_tr ks_cp ss_pe ss_max ss_nb ss_exp ss_norm ps_tr ps_cp pvs_pe vs_dve zs_out")
        (sem_o_ms, sem_o_rt, sem_o_rs, sem_fin, sem_fin_out, sem_dve_chain, sem_pool_chain) = semaphores(
            "o_ms o_rt o_rs fin fin_out dve_chain pool_chain")
        sem_w_ld = semaphore_ring("w_ld", RING)
        sem_evac = semaphore_ring("evac", 2)
        sem_ev_rdy = semaphore_ring("ev_rdy", 2)
        sem_ev_out = semaphore_ring("ev_out", 2)
        sem_nat_out = semaphore_ring("nat_out", 2)
        sem_x_ld = semaphore_ring("x_ld", 4)
        sem_z_ld = semaphore_ring("z_ld", 4)
        sem_qq_ld = semaphore_ring("qq_ld", 2)
        sem_iks_ld = semaphore_ring("iks_ld", 2)
        sem_ksk_ld = semaphore_ring("ksk_ld", 2)
        sem_ksv_ld = semaphore_ring("ksv_ld", 1)
        sem_ksm_ld = semaphore_ring("ksm_ld", 2)
        sem_fx_ld = semaphore_ring("fx_ld", 6)

        def sb(name, shape, dt=F32, stack=ctx):
            return stack.enter_context(nc.sbuf_tensor(name, shape, dt))

        act_hi = sb("act_hi", [P, KT, T_A], F32R)
        act_lo = sb("act_lo", [P, KT, T_A], F32R)
        w_raw = sb("w_raw", [P, RING, KT // 2, P])
        w_hi = sb("w_hi", [P, RING, KT // 2, P], F32R)
        w_lo = sb("w_lo", [P, RING, KT // 2, P], F32R)
        ev = sb("ev", [P, 2, T_A])
        conv = sb("conv", [P, 3072])
        c_cg, c_y, c_g = conv[:, 0:T_A], conv[:, T_A:2 * T_A], conv[:, 2 * T_A:3 * T_A]
        c_up = conv[:, 1920:1920 + 514]
        c_us = conv[:, 2440:2440 + NB * 18].rearrange("p (b t) -> p b t", b=NB)
        zr = [conv[:, T_A * i:T_A * (i + 1)] for i in range(4)]
        x_junk = [conv[:, 2048 + 512 * i:2560 + 512 * i].bitcast(BF16) for i in range(2)]
        o_junk = [conv[:, 2592 + 64 * i:2656 + 64 * i].bitcast(BF16) for i in range(5)]
        nat = sb("nat", [P, 5, P])
        gbc = sb("gbc", [P, D])
        wi_nat = sb("wi_nat", [P, 9, IH])
        wicol = sb("wicol", [P, 2, NB])
        ident = sb("ident", [P, P])
        sel = sb("sel", [P, 112 + P])
        wcv = sb("wcv", [P, 3, 8])
        st = sb("st", [P, 8, 2 * NB])
        cs = sb("cs", [P, 8, 2 + 2 * NB])
        u_prev = sb("u_prev", [P, 8, 2])
        top8 = sb("top8", [P, 8])
        o_ssq = sb("o_ssq", [P, 5, KT])
        stat = sb("stat", [P, 64])
        mx, nb_, sm, rs = (stat[:, 4 * i:4 * i + 4] for i in range(4))
        mx_s, nb_s, sm_s, rs_s = (stat[:, 16 + i:17 + i] for i in range(4))
        x_stat = [stat[:, 20 + i:21 + i] for i in range(4)]
        x_sums = stat[:, 44:46]
        o_stat = [stat[:, 24 + 5 * i:29 + 5 * i] for i in range(4)]

        attention = ExitStack()
        F = sb("F", [P, 4096], F32, attention)
        raw = sb("raw", [P, 1024], F32, attention)
        qraw = sb("qraw", [P, 1024], F32, attention)
        keys_hi = sb("keys_hi", [P, 1024], F32R, attention)
        keys_lo = sb("keys_lo", [P, 1024], F32R, attention)
        qv = sb("qv", [P, 2048], F32R, attention)
        qst = qv[:].rearrange("p (h t) -> p h t", h=IH)
        v_hi, v_lo = qv[:, 0:1024], qv[:, 1024:2048]
        isc = sb("isc", [P, 1032], F32, attention)
        msk = sb("msk", [P, 2, 1024], BF16, attention)
        q_hi = sb("q_hi", [P, 2, 512], F32R, attention)
        q_lo = sb("q_lo", [P, 2, 512], F32R, attention)
        pt_hi = sb("pt_hi", [P, 2, 512], F32R, attention)
        pt_lo = sb("pt_lo", [P, 2, 512], F32R, attention)
        sga = sb("sga", [P, 2, 512], F32, attention)
        zat = sb("zat", [P, 512], F32, attention)
        xh = [(F[:, 0:1024], F[:, 1024:2048]), (F[:, 2048:3072], F[:, 3072:4096]),
              (conv[:, 0:1024], conv[:, 1024:2048]), (raw[:], qraw[:])]
        qs_v = F[0:ID, 0:2048].rearrange("p (b h q) -> p b h q", b=NB, h=IH)
        iknat = F[:, 2048:2560].rearrange("p (s t d) -> p s t d", s=2, t=4)
        ikt, r_s = F[0:ID, 2560:2560 + KEYS_S], F[:, 3088:3088 + KEYS_S]
        ik_new = F[0:ID, 3616:3616 + P]
        knat = F[:, :].rearrange("p (t x) -> p t x", t=4)[:, :, 512:768]
        kts = F[:, 768:768 + 2048].rearrange("p (k x) -> p k x", k=2)[:, :, 0:KEYS_S]
        p_s, vs_new = F[:, 2816:2816 + KEYS_S], F[0:NS, 3840:4096]
        vs = sga[:].rearrange("p u (t e) -> p (u t) e", t=2)
        pts = isc[:, 0:640].rearrange("p (t n) -> p t n", t=5)
        k_new = isc[:, 640:896].rearrange("p (k t) -> p k t", k=2)
        z_s = raw[:].rearrange("p (h t) -> p h t", h=8)
        p_all = F[:, :].rearrange("p (h s) -> p h s", h=4)
        attention.close()
        o_nat = sb("o_nat", [P, 4, D])
        fin_o = sb("fin_o", [P, 2, D])
        fin_x = sb("fin_x", [P, 2, D])

        ps = ctx.enter_context(nc.psum_tensor("ps", [P, 8, 512], F32))
        block = ctx.enter_context(nc.Block())

        def tile_view(n):
            a = 2 * (n % 2)
            if TILES[n][0] == "A":
                return ps[:, a:a + 2, 0:T_A // 2], lambda t: t[:, 0:T_A].rearrange("p (a n) -> p a n", a=2)
            return ps[:, a, 0:T_B], lambda t: t[:, 0:T_B]

        def score_view(bank, b):
            k, c = pieces(b)
            return ps[:, bank:bank + k, 0:c], lambda t: t[:, 0:k * c].rearrange("p (a n) -> p a n", a=k)

        def residual(i):
            return (fin_x if i < 7 else fin_o)[:, i % 2]

        def ev_free(e):
            old = EV_TILE[e - 2]
            return 16 * EV_SPILLS[old][e % 2], turned_before(old + 1)

        @block.sync
        def _(sp):
            def spilled(group, kind, index):
                done = EV_SPILLS[tile_number(group, kind, index)]
                sp.wait_ge(sem_ev_out[0], 16 * done[0])
                sp.wait_ge(sem_ev_out[1], 16 * done[1])

            def load_weights(h):
                if h < 2 * NT:
                    sp.wait_ge(sem_w_lo, max(h - RING + 1, 0))
                    _, kind, _, col = TILES[h // 2]
                    src = (w_out_v if kind == "o" else w_in_v)[:, KT // 2 * (h % 2):KT // 2 * (h % 2 + 1), col:col + P]
                    sp.dma_start(w_raw[:, h % RING], src).then_inc(sem_w_ld[h % RING], 16)

            def load_x(i):
                buf = xh[i % 5 % 4] if i < 5 else xh[i - 5]
                slot = i % 5 % 4 if i < 5 else i - 5
                if i == 4:
                    sp.wait_ge(sem_x_read, 1)
                if i in (5, 6):
                    sp.wait_ge(sem_sel_pe, 2 * NB)
                if i == 7:
                    sp.wait_ge(sem_gb_used, 8)
                if i == 8:
                    sp.wait_ge(sem_ik_lo, 1)
                    sp.wait_ge(sem_qi_lo, QI_A)
                rows = token_rows(x_prompt[0], xs, i)
                for c in range(2):
                    sp.dma_start(buf[c], rows[:, 1024 * c:1024 * (c + 1)]).then_inc(sem_x_ld[slot], 16)

            def load_z(g, k):
                m = k + KT * g
                group = "AB"[g]
                if k == 0:
                    sp.wait_ge(sem_z_out, 16 * (UNITS_A, UNITS)[g])
                    sp.wait_ge(sem_zs_out, 16)
                    spilled(group, "gb", 7)
                    sp.wait_ge(sem_gb_used, 16)
                sp.wait_ge(sem_z_lo, max(m - 3, 0))
                sp.dma_start(zr[m % 4][:, 0:TOKENS[group]],
                             z_mix[P * k:P * (k + 1), COLUMN[group]:COLUMN[group] + TOKENS[group]]
                             ).then_inc(sem_z_ld[m % 4], 16)

            def spill(n):
                group, kind, index, _ = TILES[n]
                e, t, c = EV[n], TOKENS[group], COLUMN[group]
                sp.wait_ge(sem_ev_rdy[e % 2], e // 2 + 1)
                sp.dma_start(spill_to[kind][P * index:P * (index + 1), c:c + t], ev[:, e % 2, 0:t]
                             ).then_inc(sem_ev_out[e % 2], 16)

            def store_turned(n):
                group, kind, index, _ = TILES[n]
                if kind == "o" and group == "B":
                    return
                sp.wait_ge(sem_nat_cp, TURN[n] + 1)
                if kind == "o":
                    sp.dma_start(z_og[:, P * index:P * (index + 1)].rearrange("(i p) d -> p i d", p=P), nat[:]
                                 ).then_inc(sem_nat_out[0], 16)
                    return
                rows = slice(0, 512) if group == "A" else slice(512, 1024)
                dst_p, dst_s, w = {"kiwi": (new_ik_p[0, 0], new_ik_s[0], ID),
                                   "k": (new_k_p[0, 0][:, index], new_k_s[0][:, :, index], P),
                                   "v": (new_v_p[0, 0][:, index], new_v_s[0][:, :, index], P)}[kind]
                sp.dma_start(dst_p[rows].rearrange("(i p) d -> p i d", p=P), nat[:, 0:4, 0:w]
                             ).then_inc(sem_nat_out[0], 16)
                if group == "A":
                    sp.dma_start(dst_s.rearrange("b t d -> (b t) d"), nat[:, 4, 0:w]).then_inc(sem_nat_out[1], 16)

            def key_columns(z, group):
                return [z[:, 0:512]] if group == "A" else [z[:, 0:512], z[:, T_A:T_A + 512]]

            def index_loads(step):
                kind, n = step[0], NTH[step]
                if kind == "IK":
                    group = step[1]
                    spilled(group, "kiwi", 0)
                    if group == "A":
                        sp.wait_ge(sem_x_read, 5)
                    else:
                        sp.wait_ge(sem_vv_lo, 2)
                        sp.wait_ge(sem_zs_out, 16)
                    for half in range(2):
                        for c, src in enumerate(key_columns(z_kiwi[0:ID], group)):
                            sp.dma_start(raw[ID * half:ID * half + ID, 512 * c:512 * c + 512], src
                                         ).then_inc(sem_ik_ld, 16)
                elif kind == "QI":
                    _, b, half = step
                    spilled(group_of(b), "qi", 7)
                    sp.wait_ge(sem_qi_lo, n)
                    if n == 0:
                        sp.wait_ge(sem_x_read, 5)
                    if n == QI_A:
                        sp.wait_ge(sem_qq_lo, UNITS_A)
                        sp.wait_ge(sem_ss_pe, NB)
                    src = z_qi[:, block_column(b):block_column(b) + P].rearrange("(h d) t -> d h t", d=ID)
                    for r in range(2):
                        sp.dma_start(qraw[ID * r:ID * r + ID, :].rearrange("p (h t) -> p h t", h=8),
                                     src[:, 8 * half:8 * half + 8]).then_inc(sem_qi_ld, 16)
                elif kind == "QS":
                    spilled("A", "qi", 7)
                    sp.wait_ge(sem_x_read, 5)
                    for b in range(NB):
                        c = 512 + NS * b
                        sp.dma_start(qs_v[:, b], z_qi[:, c:c + NS].rearrange("(h d) q -> d h q", d=ID)
                                     ).then_inc(sem_qs_ld, 16)
                    for j in range(2):
                        for h in range(8):
                            row = ID + 8 * j + h
                            src = z_kiwi[row:row + 1, 512:T_A].rearrange("o (b q) -> (o q) b", q=NS)
                            sp.dma_start(wicol[NS * h:NS * h + NS, j], src, allow_slow_non_contiguous=True
                                         ).then_inc(sem_qs_ld, 16)
                    sp.dma_start(ik_new, z_kiwi[0:ID, 512:T_A]).then_inc(sem_qs_ld, 16)
                elif kind == "IKS":
                    b = step[1]
                    sp.wait_ge(sem_x_read, 5)
                    sp.wait_ge(sem_iks_tr, max(b - 1, 0))
                    sp.dma_start(iknat[:, b % 2], cache_idx_k[0, b].rearrange("(t p) d -> p t d", p=P)
                                 ).then_inc(sem_iks_ld[b % 2], 16)

            def softmax_loads(step):
                kind, n = step[0], NTH[step]
                if kind == "KK":
                    _, group, kv = step
                    spilled(group, "k", 1)
                    sp.wait_ge(sem_vv_lo, n)
                    sp.wait_ge(sem_ik_lo, 1 if group == "A" else 2)
                    sp.wait_ge(sem_x_read, 9)
                    for c, src in enumerate(key_columns(z_k[P * kv:P * kv + P], group)):
                        sp.dma_start(raw[:, 512 * c:512 * c + 512], src).then_inc(sem_kk_ld, 16)
                elif kind == "VV":
                    _, group, kv = step
                    nt = 4 if group == "A" else 8
                    sp.wait_ge(sem_nat_out[0], 16 * (TURN[tile_number(group, "v", 1)] + 1))
                    sp.wait_ge(sem_kk_lo, n + 1)
                    sp.dma_start(raw[:, 0:P * nt].rearrange("p (t d) -> p t d", t=nt),
                                 new_v_p[0, 0][0:P * nt, kv].rearrange("(t p) d -> p t d", p=P)
                                 ).then_inc(sem_vv_ld, 16)
                elif kind == "QQ":
                    _, b, kv = step
                    u, c, w = n % 2, block_column(b), P * (b + 1)
                    spilled(group_of(b), "ga", 3 + 4 * kv)
                    sp.wait_ge(sem_mask_out, 16 * (MASKS_A if b < 4 else len(MASKS)))
                    sp.wait_ge(sem_qi_lo, QI_A if b < 4 else QI_ALL)
                    sp.wait_ge(sem_x_read, 9)
                    sp.wait_ge(sem_qq_lo, max(n - 1, 0))
                    sp.wait_ge(sem_z_dve, max(n - 1, 0))
                    sp.wait_ge(sem_s_max, 4 * max(n - 1, 0))
                    if n >= UNITS_A:
                        sp.wait_ge(sem_ss_max, NB)
                        sp.wait_ge(sem_pvs_pe, NB)
                    sp.dma_start(qraw[:, 512 * u:512 * u + 512].rearrange("p (h t) -> p h t", h=4),
                                 z_q[512 * kv:512 * kv + 512, c:c + P].rearrange("(h d) t -> d h t", d=P)
                                 ).then_inc(sem_qq_ld[u], 16)
                    sp.dma_start(sga[:, u].rearrange("p (h t) -> p h t", h=4),
                                 z_ga[512 * kv:512 * kv + 512, c:c + P].rearrange("(h d) t -> d h t", d=P)
                                 ).then_inc(sem_qq_ld[u], 16)
                    sp.dma_start(msk[:, u, 0:w], z_mask[P * b:P * b + P, 0:w]).then_inc(sem_qq_ld[u], 16)
                elif kind == "QQS":
                    sp.wait_ge(sem_qq_lo, UNITS_A)
                    sp.wait_ge(sem_vv_lo, 2)
                    for b in range(NB):
                        c = 512 + NS * b
                        sp.dma_start(qraw[:, P * b:P * b + P].rearrange("p (h q) -> p h q", h=8),
                                     z_q[:, c:c + NS].rearrange("(h d) q -> d h q", d=P)).then_inc(sem_qqs_ld, 16)
                    sp.dma_start(z_s, z_ga[:, 512:T_A].rearrange("(h d) t -> d h t", d=P)).then_inc(sem_qqs_ld, 16)
                    sp.dma_start(k_new, z_k[:, 512:T_A].rearrange("(k d) t -> d k t", d=P)).then_inc(sem_qqs_ld, 16)
                elif kind == "KS":
                    b = step[1]
                    sp.wait_ge(sem_x_read, 9)
                    sp.wait_ge(sem_ks_tr, b)
                    sp.dma_start(knat, cache_k[0, b].rearrange("(t p) k d -> p t (k d)", p=P)
                                 ).then_inc(sem_ksk_ld[b % 2], 16)
                    sp.wait_ge(sem_s_max, 4 * UNITS_A)
                    sp.wait_ge(sem_ss_max, max(b - 1, 0))
                    for h in range(8):
                        sp.dma_start(msk[NS * h:NS * h + NS, b % 2, 0:KEYS_S],
                                     z_mask[8 * P + NS * b:8 * P + NS * (b + 1), 0:KEYS_S]
                                     ).then_inc(sem_ksm_ld[b % 2], 16)
                elif kind == "SS":
                    b = step[1]
                    sp.wait_ge(sem_pvs_pe, b)
                    sp.wait_ge(sem_z_dve, UNITS_A)
                    sp.wait_ge(sem_pt_pe, PT_A)
                    sp.dma_start(vs[:, 0:4], cache_v[0, b].rearrange("(t p) k d -> p t (k d)", p=P)
                                 ).then_inc(sem_ksv_ld[0], 16)
                    sp.dma_start(vs_new, new_v_s[0, b].rearrange("t k d -> t (k d)")
                                 ).then_inc(sem_ksv_ld[0], 16)

            def stores(step):
                kind, n = step[0], NTH[step]
                if kind == "CHUNKS" or (kind == "TK" and last_rounds(step)):
                    b = step[1]
                    m = MASKS.index(b)
                    w, r = (KEYS_S, 8 * P) if b == "s" else (P * (b + 1), P * b)
                    sp.wait_ge(sem_mask, m + 1)
                    sp.dma_start(z_mask[r:r + P, 0:w], msk[:, 0, 0:w]).then_inc(sem_mask_out, 16)
                elif kind == "ZZ":
                    _, b, kv = step
                    c = block_column(b)
                    sp.wait_ge(sem_z_dve, n + 1)
                    sp.dma_start(z_mix[512 * kv:512 * kv + 512, c:c + P].rearrange("(h d) t -> d h t", d=P),
                                 zat[:].rearrange("p (h t) -> p h t", h=4)).then_inc(sem_z_out, 16)
                elif kind == "ZS":
                    sp.wait_ge(sem_vs_dve, NB)
                    sp.dma_start(z_mix[0:1024, 512:T_A].rearrange("(h d) t -> d h t", d=P), z_s
                                 ).then_inc(sem_zs_out, 16)
                elif kind == "FIN":
                    i = step[1]
                    src = fin_o[:, i % 2] if i < 5 else o_nat[:, i - 5]
                    for c in range(2):
                        cut = slice(D // 2 * c, D // 2 * (c + 1))
                        sp.wait_ge(sem_fin, 2 * n + c + 1)
                        sp.dma_start(token_rows(y_prompt[0], ys, i)[:, cut], src[:, cut]).then_inc(sem_fin_out, 16)

            def load_final(i):
                sp.wait_ge(sem_z_out, 16 * UNITS)
                sp.wait_ge(sem_z_lo, 2 * KT)
                sp.wait_ge(sem_fin, 2 * min(max(i - 1, 0), 5))
                sp.wait_ge(sem_fin_out, 32 * (max(i - 1, 0) if i < 5 else i - 3 if i > 6 else 0))
                if i < 5:
                    sp.wait_ge(sem_nat_out[0], 16 * turned_before(OUT_B))
                    sp.dma_start(fin_o[:, i % 2], z_og[P * i:P * (i + 1)]).then_inc(sem_fx_ld[final_slot(i)], 16)
                sp.dma_start(residual(i), token_rows(x_prompt[0], xs, i)).then_inc(sem_fx_ld[final_slot(i)], 16)

            load_x(0)
            sp.dma_start(gbc[:], g_pre[0:1, :].broadcast_to([P, D])).then_inc(sem_g_ld, 16)
            for i in range(1, 4):
                load_x(i)
            load_weights(0)
            load_weights(1)
            load_x(4)
            load_weights(2)
            for j in range(3):
                sp.dma_start(wcv[:, j], w_conv[0, j].rearrange("(c p) -> p c", p=P),
                             allow_slow_non_contiguous=True).then_inc(sem_wcv_ld, 16)
            for c in range(8):
                sp.dma_start(st[:, c], state_conv[0][:, :, P * c:P * (c + 1)].rearrange("b j p -> p (b j)"),
                             allow_slow_non_contiguous=True).then_inc(sem_st_ld, 16)

            for slot in range(TAIL + 1):
                n, s = divmod(slot, SLOTS)
                if n < NT and s in (0, 4):
                    load_weights(2 * n + s // 4 + RING)
                if slot:
                    for step in SIDE.get(slot - 1, ()):
                        stores(step)
                for step in LOADS.get(slot, ()):
                    index_loads(step)
                    softmax_loads(step)
                    if step[0] == "NX":
                        load_x(step[1])
                    if step[0] == "FIN":
                        load_final(step[1])
                for g in range(2):
                    if n == PHASE_LAST[1 + g]:
                        for k in range(KT):
                            if s == max(0, (k - 4) // 2):
                                load_z(g, k)
                if n and s == 2 and TILES[n - 1][1] in SPILLED:
                    spill(n - 1)
                if n and s == 4 and TILES[n - 1][1] in TURNED:
                    store_turned(n - 1)
                if slot == SLOTS * NP + 16:
                    sp.wait_ge(sem_x_rdy, 9)
                    sp.dma_start(gbc[:], g_post[0:1, :].broadcast_to([P, D])).then_inc(sem_g_ld, 16)
                if slot == SLOTS * (OUT_A + 2):
                    sp.wait_ge(sem_hc_rdy, 16)
                    for c in range(8):
                        part = slice(P * c, P * c + P)
                        sp.dma_start(conv_p[0, 0][:, part].rearrange("j p -> p j"), cs[:, c, 0:2],
                                     allow_slow_non_contiguous=True).then_inc(sem_cs_out, 16)
                        sp.dma_start(conv_s[0][:, :, part].rearrange("b j p -> p (b j)"), cs[:, c, 2:2 + 2 * NB],
                                     allow_slow_non_contiguous=True).then_inc(sem_cs_out, 16)
                if slot == SLOTS * (NT - 1):
                    for i in range(5, 9):
                        load_final(i)
            for step in SIDE[TAIL]:
                stores(step)
            sp.wait_ge(sem_cs_out, 16 * 16)
            sp.wait_ge(sem_fin_out, 32 * 9)
            sp.wait_ge(sem_nat_out[0], 16 * turned_before(OUT_B))
            sp.wait_ge(sem_nat_out[1], 16 * turned_before(NP))
            sp.wait_ge(sem_mask_out, 16 * len(MASKS))
            sp.wait_ge(sem_z_out, 16 * UNITS)
            sp.wait_ge(sem_zs_out, 16)
            spilled("B", "ga", 7)

        @block.gpsimd
        def _(pool):
            chain = [0]

            def link(ins):
                chain[0] += 1
                ins.then_inc(sem_pool_chain, 1)
                pool.wait_ge(sem_pool_chain, chain[0])

            def split_low(h):
                if h < 2 * NT:
                    pool.wait_ge(sem_w_hi, h + 1)
                    r = h % RING
                    nc.gpsimd.tensor_tensor(w_lo[:, r], w_raw[:, r], w_hi[:, r].bitcast(F32), ALU.subtract
                                            ).then_inc(sem_w_lo, 1)

            link(nc.gpsimd.memset(ident[:], 0.0))
            link(nc.gpsimd.affine_select(out=ident[:], in_=ident[:], compare_op=ALU.not_equal, fill=1.0, base=0,
                                         pattern=[[-1, P]], channel_multiplier=1))
            link(nc.gpsimd.memset(sel[:], 0.0))
            own = sel[:, 112:112 + NS]
            for h in range(8):
                link(nc.gpsimd.affine_select(out=own, in_=own, compare_op=ALU.not_equal, fill=1.0, base=-NS * h,
                                             pattern=[[-1, NS]], channel_multiplier=1))
            pool.sem_inc(sem_const, 1)
            for h in range(RING + 2 * NT):
                split_low(h)

        @block.tensor
        def _(pe):
            def transpose(out, in_):
                return nc.tensor.transpose(out, in_, ident[0:in_.shape[0], 0:in_.shape[0]])

            def norm_unit(m):
                i, j = UNITS_X[m]
                pe.wait_ge(sem_x_rdy, i + 1)
                pe.wait_ge(sem_x_lo, max(m - 3, 0))
                if m == NX_A:
                    pe.wait_ge(sem_iscs, 1)
                    pe.wait_ge(sem_isum, HEADS_A)
                    pe.wait_ge(sem_hs_r, 2 * NB)
                half = xh[i % 5 % 4 if i < 5 else i - 5][j // 2]
                for r in range(4):
                    c = P * (4 * (j % 2) + r)
                    last = transpose(ps[:, 4 + m % 4, P * r:P * r + P], half[:, c:c + P])
                last.then_inc(sem_x_tr, 1)
                if j == 3:
                    pe.wait_ge(sem_x_tr, m + 1)
                    pe.sem_inc(sem_x_read, 1)

            def gemm(n, s):
                group = TILES[n][0]
                count = 2 if group == "A" else 1
                w = TOKENS[group] // count
                bank = 2 * (n % 2)
                if s == 0:
                    pe.wait_ge(sem_evac[n % 2], n // 2)
                if s % 4 == 0:
                    pe.wait_ge(sem_w_lo, 2 * n + s // 4 + 1)
                if n == 0 and s == 0:
                    pe.wait_ge(sem_x_lo, NX_A)
                for k in range(PER * s, PER * (s + 1)):
                    if n == NP and k % 4 == 0:
                        pe.wait_ge(sem_x_lo, NX_A + k + 4)
                    if n in (OUT_A, OUT_B):
                        pe.wait_ge(sem_z_lo, k + 1 + KT * (n == OUT_B))
                    r = (2 * n + k // 8) % RING
                    for wt, parts in ((w_hi, (act_hi, act_lo)), (w_lo, (act_hi,))):
                        for a in parts:
                            for x in range(count):
                                last = nc.tensor.matmul(ps[:, bank + x, 0:w], wt[:, r, k % 8], a[:, k, w * x:w * (x + 1)],
                                                        start=(k == 0 and wt is w_hi and a is act_hi),
                                                        stop=(k == KT - 1 and wt is w_lo))
                if s % 4 == 3:
                    last.then_inc(sem_gemm, 1)
                elif n in PHASE_LAST[:3]:
                    last.then_inc(sem_passed, 1)

            def turn(n):
                e, a = EV[n], 2 * (n % 2)
                pe.wait_ge(sem_ev_rdy[e % 2], e // 2 + 1)
                for i in range(TT[TILES[n][0]]):
                    last = transpose(ps[:, a + i // 4, P * (i % 4):P * (i % 4) + P], ev[:, e % 2, P * i:P * i + P])
                last.then_inc(sem_nat_pe, 1)

            def score_product(b, bank, operands):
                k, c = pieces(b)
                for x in range(k):
                    for i, (lhs, rhs) in enumerate(operands):
                        last = nc.tensor.matmul(ps[:, bank + x, 0:c], lhs, rhs[:, c * x:c * (x + 1)],
                                                start=(i == 0), stop=(i == len(operands) - 1))
                return last

            def index_step(step):
                kind, n = step[0], NTH[step]
                if kind == "HEAD":
                    _, b, hp = step
                    pe.wait_ge(sem_ik_lo, NTH["IK", group_of(b)] + 1)
                    pe.wait_ge(sem_qi_lo, NTH["QI", b, hp // 4] + 1)
                    if n == HEADS_A // 2:
                        pe.wait_ge(sem_z_dve, UNITS_A)
                        pe.wait_ge(sem_pt_lo, PT_A)
                        pe.wait_ge(sem_ps_cp, NB)
                        pe.wait_ge(sem_vs_dve, NB)
                    for odd in range(2):
                        pe.wait_ge(sem_isum, max(2 * n - 1 + odd, 0))
                        q = qst[:, 2 * hp + odd]
                        score_product(b, 4 + 2 * odd, ((q, keys_hi), (q, keys_lo))).then_inc(sem_head_pe, 1)
                elif kind == "IKS":
                    b = step[1]
                    pe.wait_ge(sem_iks_ld[b % 2], 16 * (b // 2 + 1))
                    pe.wait_ge(sem_isum, HEADS_A)
                    pe.wait_ge(sem_hs_r, 2 * b)
                    for t in range(4):
                        last = transpose(ps[0:ID, 4, P * t:P * t + P], iknat[:, b % 2, t])
                    last.then_inc(sem_iks_tr, 1)
                elif kind == "HS":
                    _, b, j = step
                    pe.wait_ge(sem_iks_cp, b + 1)
                    pe.wait_ge(sem_qs_ld, 16 * 25)
                    pe.wait_ge(sem_hs_r, n)
                    for x in range(2):
                        lhs = qs_v[:, b, 8 * j:8 * j + 8].rearrange("p h q -> p (h q)")
                        last = nc.tensor.matmul(ps[:, 4 + x, 0:HALF_S], lhs, ikt[:, HALF_S * x:HALF_S * (x + 1)],
                                                start=True, stop=True)
                    last.then_inc(sem_hs_pe, 1)
                elif kind == "SEL":
                    _, b, j = step
                    pe.wait_ge(sem_hs_r, n + 1)
                    for x in range(2):
                        last = nc.tensor.matmul(ps[:, 6 + x, 0:HALF_S], sel[:, 112 - NS * b:112 - NS * b + P],
                                                r_s[:, HALF_S * x:HALF_S * (x + 1)], start=(n == 0), stop=(n == 2 * NB - 1))
                    last.then_inc(sem_sel_pe, 1)

            def value_product(p, j, count):
                pe.wait_ge(sem_pt_lo, p + 1)
                for i, (lhs, rhs) in enumerate(((v_hi, pt_hi), (v_hi, pt_lo), (v_lo, pt_hi))):
                    last = nc.tensor.matmul(ps[:, 4, :], lhs[:, P * j:P * j + P], rhs[:, p % 2],
                                            start=(j == 0 and i == 0), stop=(j == count - 1 and i == 2))
                last.then_inc(sem_pv_pe, 1)

            def softmax_step(step):
                kind, n = step[0], NTH[step]
                if kind == "S":
                    _, b, kv, h = step
                    u = NTH["QQ", b, kv]
                    pe.wait_ge(sem_qq_lo, u + 1)
                    pe.wait_ge(sem_kk_lo, NTH["KK", group_of(b), kv] + 1)
                    pe.wait_ge(sem_s_max, max(n - 1, 0))
                    pe.wait_ge(sem_z_dve, u)
                    pe.wait_ge(sem_pt_lo, before(step, "PT"))
                    if n == 0:
                        pe.wait_ge(sem_x_lo, NX_A + NX_B)
                    if n == 4 * UNITS_A:
                        pe.wait_ge(sem_isum, HEADS)
                    hi, lo = q_hi[:, u % 2, P * h:P * h + P], q_lo[:, u % 2, P * h:P * h + P]
                    score_product(b, 4 + 2 * (h % 2), ((hi, keys_hi), (hi, keys_lo), (lo, keys_hi))).then_inc(sem_s_pe, 1)
                elif kind == "PT":
                    _, b, kv, j = step
                    u = NTH["QQ", b, kv]
                    pe.wait_ge(sem_s_norm, 4 * (u + 1))
                    pe.wait_ge(sem_vv_lo, NTH["VV", group_of(b), kv] + 1)
                    pe.wait_ge(sem_pt_lo, max(n - 1, 0))
                    for h in range(4):
                        last = transpose(ps[:, 6 + n % 2, P * h:P * h + P], p_all[:, h, P * j:P * j + P])
                    last.then_inc(sem_pt_pe, 1)
                    if j > 0:
                        value_product(n - 1, j - 1, b + 1)
                elif kind == "ZZ":
                    b = step[1]
                    value_product(before(step, "PT") - 1, b, b + 1)
                elif kind == "KS":
                    b = step[1]
                    pe.wait_ge(sem_ksk_ld[b % 2], 16 * (b // 2 + 1))
                    pe.wait_ge(sem_z_dve, UNITS_A)
                    pe.wait_ge(sem_ps_cp, max(b - 1, 0))
                    for kv in range(2):
                        for t in range(4):
                            last = transpose(ps[:, 4 + kv, P * t:P * t + P], knat[:, t, P * kv:P * kv + P])
                    last.then_inc(sem_ks_tr, 1)
                elif kind == "SS":
                    b = step[1]
                    pe.wait_ge(sem_ks_cp, b + 1)
                    pe.wait_ge(sem_qqs_ld, 16 * (NB + 2))
                    pe.wait_ge(sem_vs_dve, b)
                    pe.wait_ge(sem_pt_lo, PT_A)
                    for kv in range(2):
                        for x in range(2):
                            last = nc.tensor.matmul(ps[64 * kv:64 * kv + 64, 6 + x, 0:HALF_S],
                                                    qraw[:, P * b + 64 * kv:P * b + 64 * kv + 64],
                                                    kts[:, kv, HALF_S * x:HALF_S * (x + 1)], start=True, stop=True)
                    last.then_inc(sem_ss_pe, 1)
                elif kind == "PS":
                    b = step[1]
                    pe.wait_ge(sem_ss_norm, b + 1)
                    pe.wait_ge(sem_ks_cp, min(b + 2, NB))
                    for t in range(4):
                        transpose(ps[:, 4, P * t:P * t + P], p_s[:, P * t:P * t + P])
                    transpose(ps[0:NS, 5, 0:P], p_s[:, PAST:KEYS_S]).then_inc(sem_ps_tr, 1)
                elif kind == "VS":
                    b = step[1]
                    pe.wait_ge(sem_ps_cp, b + 1)
                    pe.wait_ge(sem_ksv_ld[0], 32 * (b + 1))
                    pe.wait_ge(sem_ss_max, b + 1)
                    for kv in range(2):
                        for t in range(5):
                            r = P if t < 4 else NS
                            v = (vs[:, t] if t < 4 else vs_new)[:, P * kv:P * kv + P]
                            last = nc.tensor.matmul(ps[:, 6, 64 * kv:64 * kv + 64], v,
                                                    pts[0:r, t, 64 * kv:64 * kv + 64], start=(t == 0), stop=(t == 4))
                    last.then_inc(sem_pvs_pe, 1)

            pe.wait_ge(sem_const, 1)
            for m in range(NX_A):
                norm_unit(m)
            for slot in range(TAIL):
                n, s = divmod(slot, SLOTS)
                gemm(n, s)
                if n and s == 1 and TILES[n - 1][1] in TURNED:
                    turn(n - 1)
                if n == NP - 1 and s % 2:
                    for i in range(4):
                        norm_unit(NX_A + 2 * (s - 1) + i)
                for step in SIDE.get(slot, ()):
                    index_step(step)
                    softmax_step(step)
            turn(NT - 1)

        @block.scalar
        def _(act):
            def copy(out, in_):
                return nc.scalar.activation(out, in_, ACT.Copy)

            def split_high(h):
                if h < 2 * NT:
                    act.wait_ge(sem_w_ld[h % RING], 16 * (h // RING + 1))
                    act.wait_ge(sem_gemm, max(h - RING + 1, 0))
                    copy(w_hi[:, h % RING], w_raw[:, h % RING]).then_inc(sem_w_hi, 1)

            def squares(i):
                slot = i % 5 % 4 if i < 5 else i - 5
                act.wait_ge(sem_x_ld[slot], 32 * (1 + (i >= 4) + (i >= 5 and slot == 0)))
                act.wait_ge(sem_x_rdy, i)
                a, b = xh[slot]
                if i == 5:
                    act.wait_ge(sem_gb_used, 8)
                nc.scalar.activation(x_junk[0], a, ACT.Square, accum_out=x_sums[:, 0:1])
                nc.scalar.activation(x_junk[1], b, ACT.Square, accum_out=x_sums[:, 1:2]).then_inc(sem_x_ssq, 1)
                act.wait_ge(sem_x_ms, i + 1)
                nc.scalar.activation(x_stat[2], x_stat[1], ACT.Sqrt).then_inc(sem_x_rt, 1)

            def unit_high(m):
                i, j = UNITS_X[m]
                t = P * (i if i < 5 else i - 5)
                act.wait_ge(sem_x_tr, m + 1)
                if m >= NX_A:
                    passed(0, 4 * j + 3)
                copy(act_hi[:, 4 * j:4 * j + 4, t:t + P], ps[:, 4 + m % 4].rearrange("p (r t) -> p r t", r=4)
                     ).then_inc(sem_x_hi, 1)

            def passed(phase, k):
                s = k // PER
                if s == SLOTS - 1:
                    act.wait_ge(sem_gemm, 2 * PHASE_LAST[phase] + 2)
                elif s == 3:
                    act.wait_ge(sem_gemm, 2 * PHASE_LAST[phase] + 1)
                else:
                    act.wait_ge(sem_passed, 6 * phase + s + 1 - (s > 3))

            def z_high(g, k):
                m, t = k + KT * g, TOKENS["AB"[g]]
                passed(1 + g, k)
                act.wait_ge(sem_z_ld[m % 4], 16 * (m // 4 + 1))
                copy(act_hi[:, k, 0:t], zr[m % 4][:, 0:t]).then_inc(sem_z_hi, 1)

            def evacuate(n):
                group, kind, index, _ = TILES[n]
                src, like = tile_view(n)
                c = index + 8 * (group == "B")
                act.wait_ge(sem_gemm, 2 * n + 2)
                if kind in BUFFERED and kind != "gb":
                    e = EV[n]
                    if e >= 2:
                        out, turned = ev_free(e)
                        act.wait_ge(sem_ev_out[e % 2], out)
                        act.wait_ge(sem_nat_pe, turned)
                    nc.scalar.activation(like(ev[:, e % 2]), src, ACT.Silu if kind == "ga" else ACT.Copy
                                         ).then_inc(sem_ev_rdy[e % 2], 1)
                    if kind not in TURNED:
                        act.wait_ge(sem_ev_rdy[e % 2], e // 2 + 1)
                        act.sem_inc(sem_evac[n % 2], 1)
                elif kind == "cg":
                    act.wait_ge(sem_hc_rdy, c)
                    copy(like(c_cg), src).then_inc(sem_cg_rdy, 1)
                    act.wait_ge(sem_cg_rdy, c + 1)
                    act.sem_inc(sem_evac[n % 2], 1)
                elif kind == "gb":
                    act.wait_ge(sem_gb_used, c)
                    nc.scalar.activation(like(c_g), src, ACT.Silu).then_inc(sem_gb_silu, 1)
                    act.wait_ge(sem_gb_silu, c + 1)
                    act.sem_inc(sem_evac[n % 2], 1)

            def turned_squares(n):
                a = 2 * (n % 2)
                act.wait_ge(sem_nat_cp, TURN[n] + 1)
                if TILES[n][:3] == ("B", "o", 0):
                    act.wait_ge(sem_o_ms, 1)
                for i in range(TT[TILES[n][0]]):
                    last = nc.scalar.activation(o_junk[i], ps[:, a + i // 4, P * (i % 4):P * (i % 4) + P], ACT.Square,
                                                accum_out=o_ssq[:, i, TILES[n][2]:TILES[n][2] + 1])
                last.then_inc(sem_nat_sq, 1)
                act.wait_ge(sem_nat_sq, TURN[n] - TURN[OUT_A] + 1)
                act.sem_inc(sem_evac[n % 2], 1)

            def index_step(step):
                kind, n = step[0], NTH[step]
                if kind == "IK":
                    w = 512 if step[1] == "A" else 1024
                    act.wait_ge(sem_ik_ld, 32 if step[1] == "A" else 96)
                    if step[1] == "B":
                        act.wait_ge(sem_s_pe, 4 * UNITS_A)
                    copy(keys_hi[:, 0:w], raw[:, 0:w]).then_inc(sem_ik_hi, 1)
                elif kind == "QI":
                    act.wait_ge(sem_qi_ld, 32 * (n + 1))
                    act.wait_ge(sem_head_pe, 2 * before(step, "HEAD"))
                    if step[1] >= 4:
                        act.wait_ge(sem_pv_pe, PT_A)
                    copy(qv[:, 1024 * step[2]:1024 * step[2] + 1024], qraw[:]).then_inc(sem_qi_hi, 1)
                elif kind == "HEAD":
                    for odd in range(2):
                        act.wait_ge(sem_head_pe, 2 * n + 1 + odd)
                        v, _ = score_view(4 + 2 * odd, step[1])
                        nc.scalar.activation(v, v, ACT.Relu, scale=(ID * IH * 1.0) ** -0.5).then_inc(sem_relu, 1)
                elif kind == "IKS":
                    b = step[1]
                    act.wait_ge(sem_iks_tr, b + 1)
                    act.wait_ge(sem_hs_pe, 2 * b)
                    if b == 0:
                        act.wait_ge(sem_qs_ld, 16 * 25)
                    copy(ikt[:, PAST:KEYS_S], ik_new[:, NS * b:NS * (b + 1)])
                    copy(ikt[:, 0:PAST], ps[0:ID, 4, :]).then_inc(sem_iks_cp, 1)

            def softmax_step(step):
                kind, n = step[0], NTH[step]
                if kind == "KK":
                    w = 512 if step[1] == "A" else 1024
                    act.wait_ge(sem_kk_ld, (16, 32, 64, 96)[n])
                    act.wait_ge(sem_s_pe, 16 * n)
                    act.wait_ge(sem_head_pe, HEADS_A if n < 2 else HEADS)
                    copy(keys_hi[:, 0:w], raw[:, 0:w]).then_inc(sem_kk_hi, 1)
                elif kind == "VV":
                    w = 512 if step[1] == "A" else 1024
                    act.wait_ge(sem_vv_ld, 16 * (n + 1))
                    act.wait_ge(sem_pv_pe, before(step, "PT"))
                    act.wait_ge(sem_head_pe, HEADS_A if n < 2 else HEADS)
                    copy(v_hi[:, 0:w], raw[:, 0:w]).then_inc(sem_vv_hi, 1)
                elif kind == "QQ":
                    u = n % 2
                    act.wait_ge(sem_qq_ld[u], 48 * (n // 2 + 1))
                    act.wait_ge(sem_s_pe, 4 * max(n - 1, 0))
                    copy(q_hi[:, u], qraw[:, 512 * u:512 * u + 512]).then_inc(sem_qq_hi, 1)
                elif kind == "S":
                    _, b, kv, h = step
                    act.wait_ge(sem_s_nb, n + 1)
                    p = p_all[:, h, 0:P * (b + 1)]
                    nc.scalar.activation(p, p, ACT.Exp, bias=nb_[:, h:h + 1], scale=SCALE, accum_out=sm[:, h:h + 1]
                                         ).then_inc(sem_s_exp, 1)
                elif kind == "PT":
                    act.wait_ge(sem_pt_pe, n + 1)
                    act.wait_ge(sem_pv_pe, max(n - 1, 0))
                    copy(pt_hi[:, n % 2], ps[:, 6 + n % 2]).then_inc(sem_pt_hi, 1)
                elif kind == "KS":
                    b = step[1]
                    act.wait_ge(sem_ks_tr, b + 1)
                    act.wait_ge(sem_pt_pe, PT_A)
                    act.wait_ge(sem_ss_pe, b)
                    if b == 0:
                        act.wait_ge(sem_qqs_ld, 16 * (NB + 2))
                    copy(kts[:, :, PAST:KEYS_S], k_new[:, :, NS * b:NS * (b + 1)])
                    copy(kts[:, :, 0:PAST], ps[:, 4:6]).then_inc(sem_ks_cp, 1)
                elif kind == "SS":
                    act.wait_ge(sem_ss_nb, n + 1)
                    nc.scalar.activation(p_s, p_s, ACT.Exp, bias=nb_s, scale=SCALE, accum_out=sm_s
                                         ).then_inc(sem_ss_exp, 1)
                elif kind == "PS":
                    act.wait_ge(sem_ps_tr, n + 1)
                    act.wait_ge(sem_pvs_pe, n)
                    copy(pts[:, 0:4], ps[:, 4].rearrange("p (t n) -> p t n", t=4))
                    copy(pts[0:NS, 4], ps[0:NS, 5, 0:P]).then_inc(sem_ps_cp, 1)

            def root_step(step):
                if step[0] == "RMS":
                    n = NTH[step]
                    act.wait_ge(sem_o_ms, n + 1)
                    nc.scalar.activation(o_stat[2], o_stat[1], ACT.Sqrt).then_inc(sem_o_rt, 1)

            for i in range(6):
                if i < 5:
                    squares(i)
                if i > 0:
                    for m in range(4 * (i - 1), 4 * i):
                        unit_high(m)
                if i in (3, 4):
                    split_high(i - 3)
            for slot in range(TAIL + SLOTS):
                n, s = divmod(slot, SLOTS)
                if n and s == 0:
                    evacuate(n - 1)
                if n < NT and s in (0, 4):
                    split_high(2 * n + s // 4 + RING - 1)
                if n and s == 2 and TILES[n - 1][1] == "o":
                    turned_squares(n - 1)
                if n == NP - 1 and s % 2:
                    for i in range(4):
                        unit_high(NX_A + 2 * (s - 1) + i)
                for g in range(2):
                    if n == PHASE_LAST[1 + g]:
                        z_high(g, 2 * s)
                        z_high(g, 2 * s + 1)
                if slot < TAIL:
                    for step in SIDE.get(slot, ()):
                        index_step(step)
                        softmax_step(step)
                        root_step(step)
                        if step[0] == "NX":
                            squares(step[1])
            root_step(("RMS", "B"))

        @block.vector
        def _(dve):
            chain = [0]

            def link(ins):
                chain[0] += 1
                ins.then_inc(sem_dve_chain, 1)
                dve.wait_ge(sem_dve_chain, chain[0])

            def low(out, x, hi):
                return nc.vector.tensor_tensor(out, x, hi.bitcast(F32), ALU.subtract)

            def inverse_root(s):
                link(nc.vector.reciprocal(s[3], s[2]))
                link(nc.vector.tensor_tensor(s[2], s[3], s[3], ALU.mult))
                link(nc.vector.tensor_tensor(s[2], s[2], s[1], ALU.mult))
                link(nc.vector.tensor_scalar(s[2], s[2], -0.5, 1.5, ALU.mult, ALU.add))
                return nc.vector.tensor_tensor(s[3], s[3], s[2], ALU.mult)

            def normalise_x(i):
                slot = i % 5 % 4 if i < 5 else i - 5
                dve.wait_ge(sem_x_ssq, i + 1)
                link(nc.vector.tensor_tensor(x_stat[0], x_sums[:, 0:1], x_sums[:, 1:2], ALU.add))
                nc.vector.tensor_scalar(x_stat[1], x_stat[0], 1.0 / D, EPS, ALU.mult, ALU.add).then_inc(sem_x_ms, 1)
                dve.wait_ge(sem_x_rt, i + 1)
                link(inverse_root(x_stat))
                if i == 0:
                    dve.wait_ge(sem_g_ld, 16)
                for c, x in enumerate(xh[slot]):
                    last = nc.vector.scalar_tensor_tensor(out=x, in0=x, scalar=x_stat[3],
                                                          in1=gbc[:, 1024 * c:1024 * (c + 1)], op0=ALU.mult, op1=ALU.mult)
                last.then_inc(sem_x_rdy, 1)

            def unit_low(m):
                i, j = UNITS_X[m]
                t = P * (i if i < 5 else i - 5)
                dve.wait_ge(sem_x_hi, m + 1)
                cut = (slice(None), slice(4 * j, 4 * j + 4), slice(t, t + P))
                low(act_lo[cut], ps[:, 4 + m % 4].rearrange("p (r t) -> p r t", r=4), act_hi[cut]).then_inc(sem_x_lo, 1)

            def z_low(g, k):
                m, t = k + KT * g, TOKENS["AB"[g]]
                dve.wait_ge(sem_z_hi, m + 1)
                low(act_lo[:, k, 0:t], zr[m % 4][:, 0:t], act_hi[:, k, 0:t]).then_inc(sem_z_lo, 1)

            def conv_input(n):
                group, _, c, _ = TILES[n]
                m, a = c + 8 * (group == "B"), 2 * (n % 2)
                if m == 0:
                    dve.wait_ge(sem_wcv_ld, 16 * 3)
                    dve.wait_ge(sem_st_ld, 16 * 8)
                dve.wait_ge(sem_gemm, 2 * n + 2)
                dve.wait_ge(sem_cg_rdy, m + 1)
                if group == "A":
                    nc.vector.memset(c_up[:, 0:2], 0.0)
                    nc.vector.tensor_copy(c_us[:, :, 0:2], st[:, c].rearrange("p (b j) -> p b j", b=NB))
                    nc.vector.tensor_tensor(c_up[:, 2:322], ps[:, a, 0:320], c_cg[:, 0:320], ALU.mult)
                    nc.vector.tensor_tensor(c_up[:, 322:514], ps[:, a + 1, 0:192], c_cg[:, 320:512], ALU.mult)
                    link(nc.vector.tensor_tensor(c_us[:, :, 2:18],
                                                 ps[:, a + 1, 192:320].rearrange("p (b t) -> p b t", b=NB),
                                                 c_cg[:, 512:640].rearrange("p (b t) -> p b t", b=NB), ALU.mult))
                    nc.vector.tensor_copy(cs[:, c, 2:18].rearrange("p (b j) -> p b j", b=NB), c_us[:, :, 16:18])
                    nc.vector.tensor_copy(u_prev[:, c], c_up[:, 512:514]).then_inc(sem_hc_rdy, 1)
                else:
                    nc.vector.tensor_copy(c_up[:, 0:2], u_prev[:, c])
                    link(nc.vector.tensor_tensor(c_up[:, 2:514], ps[:, a, 0:512], c_cg[:, 0:512], ALU.mult))
                    nc.vector.tensor_copy(cs[:, c, 0:2], c_up[:, 512:514]).then_inc(sem_hc_rdy, 1)
                dve.wait_ge(sem_hc_rdy, m + 1)
                dve.sem_inc(sem_evac[n % 2], 1)

            def conv_taps(n):
                group, _, c, _ = TILES[n]
                yp, ys_ = c_y[:, 0:512], c_y[:, 512:640].rearrange("p (b t) -> p b t", b=NB)
                parts = [(yp, lambda j: c_up[:, j:j + 512])]
                if group == "A":
                    parts.append((ys_, lambda j: c_us[:, :, j:j + NS]))
                for j in range(3):
                    w = wcv[:, j, c:c + 1]
                    for x, (y, u) in enumerate(parts):
                        if j == 0:
                            ins = nc.vector.tensor_scalar(y, u(0), w, None, ALU.mult)
                        else:
                            ins = nc.vector.scalar_tensor_tensor(out=y, in0=u(j), scalar=w, in1=y, op0=ALU.mult,
                                                                 op1=ALU.add)
                        if x == len(parts) - 1:
                            link(ins)
                src, like = tile_view(n)
                dve.wait_ge(sem_gemm, 2 * n + 2)
                link(nc.vector.tensor_tensor(like(c_y), src, like(c_y), ALU.mult))
                dve.sem_inc(sem_evac[n % 2], 1)

            def conv_gate(n):
                group, _, c, _ = TILES[n]
                t, e = TOKENS[group], EV[n]
                dve.wait_ge(sem_gb_silu, c + 8 * (group == "B") + 1)
                out, turned = ev_free(e)
                dve.wait_ge(sem_ev_out[e % 2], out)
                dve.wait_ge(sem_nat_pe, turned)
                nc.vector.tensor_tensor(ev[:, e % 2, 0:t], c_y[:, 0:t], c_g[:, 0:t], ALU.mult
                                        ).then_inc(sem_ev_rdy[e % 2], 1)
                dve.wait_ge(sem_ev_rdy[e % 2], e // 2 + 1)
                dve.sem_inc(sem_gb_used, 1)

            def turned_out(n):
                group, kind, index, _ = TILES[n]
                m, a, k = TURN[n], 2 * (n % 2), TT[TILES[n][0]]
                dve.wait_ge(sem_nat_pe, m + 1)
                first = ps[:, a].rearrange("p (i d) -> p i d", i=4)
                if (group, kind) != ("B", "o"):
                    dve.wait_ge(sem_nat_out[0], 16 * m)
                    dve.wait_ge(sem_nat_out[1], 16 * turned_before(n, "A", TURNED[:3]))
                if kind == "o":
                    if n == OUT_A:
                        dve.wait_ge(sem_g_ld, 32)
                    if n == OUT_B:
                        dve.wait_ge(sem_z_out, 16 * UNITS)
                    g = gbc[:, P * index:P * (index + 1)]
                    if group == "A":
                        nc.vector.tensor_tensor(nat[:, 4], ps[:, a + 1, 0:P], g, ALU.mult)
                    out = nat[:, 0:4] if group == "A" else o_nat[:, :, P * index:P * (index + 1)]
                    nc.vector.tensor_tensor(out, first, g.unsqueeze(1).broadcast_to([P, 4, P]), ALU.mult
                                            ).then_inc(sem_nat_cp, 1)
                    return
                if k == 5:
                    nc.vector.tensor_copy(nat[:, 4], ps[:, a + 1, 0:P])
                link(nc.vector.tensor_copy(nat[:, 0:4], first))
                if kind == "kiwi":
                    w0 = 0 if group == "A" else 5
                    link(nc.vector.tensor_copy(wi_nat[:, w0:w0 + k], nat[:, 0:k, ID:ID + IH]))
                dve.sem_inc(sem_nat_cp, 1)
                dve.sem_inc(sem_evac[n % 2], 1)

            def index_step(step):
                kind, n = step[0], NTH[step]
                if kind == "IK":
                    w = 512 if step[1] == "A" else 1024
                    dve.wait_ge(sem_ik_hi, n + 1)
                    low(keys_lo[:, 0:w], raw[:, 0:w], keys_hi[:, 0:w]).then_inc(sem_ik_lo, 1)
                elif kind == "QI":
                    dve.wait_ge(sem_qi_hi, n + 1)
                    cut = (slice(64, 128), slice(1024 * step[2], 1024 * step[2] + 1024))
                    low(qv[cut], qraw[64:128, :], qv[cut]).then_inc(sem_qi_lo, 1)
                elif kind == "HEAD":
                    _, b, hp = step
                    t = b + (b >= 4)
                    for odd in range(2):
                        dve.wait_ge(sem_relu, 2 * n + 1 + odd)
                        v, like = score_view(4 + 2 * odd, b)
                        wi = wi_nat[:, t, 2 * hp + odd:2 * hp + odd + 1]
                        if hp == 0 and odd == 0:
                            if n:
                                dve.wait_ge(sem_pvs_pe, NB if b >= 4 else 0)
                            ins = nc.vector.tensor_scalar(like(isc), v, wi, None, ALU.mult)
                        else:
                            dve.wait_ge(sem_isum, 2 * n + odd)
                            ins = nc.vector.scalar_tensor_tensor(out=like(isc), in0=v, scalar=wi, in1=like(isc),
                                                                 op0=ALU.mult, op1=ALU.add)
                        ins.then_inc(sem_isum, 1)
                elif kind == "TK":
                    _, b, r0 = step
                    w = KEYS_S + PAD_S if b == "s" else P * (b + 1)
                    if r0 == 0 and b == "s":
                        dve.wait_ge(sem_iscs, 1)
                    if r0 == 0 and b != "s":
                        dve.wait_ge(sem_isum, 2 * before(step, "HEAD"))
                        link(nc.vector.memset(isc[0:64, w - 64:w], NEG_LATER))
                    for r in range(r0, min(r0 + 2, ROUNDS_S if b == "s" else ROUNDS)):
                        link(nc.vector.max(top8[:], isc[:, 0:w]))
                        link(nc.vector.match_replace(isc[:, 0:w], top8[:], isc[:, 0:w], NEG_TAKEN))
                    if last_rounds(step):
                        dve.wait_ge(sem_mask_out, 16 * MASKS.index(b))
                        w = KEYS_S if b == "s" else w
                        link(nc.vector.tensor_scalar(msk[:, 0, 0:w], isc[:, 0:w], NEG_CUT, NEG_MASK, ALU.is_gt, ALU.mult))
                        dve.sem_inc(sem_mask, 1)
                elif kind == "CHUNKS":
                    w = P * (step[1] + 1)
                    dve.wait_ge(sem_mask_out, 16 * MASKS.index(step[1]))
                    link(nc.vector.memset(msk[:, 0, 0:w], 0.0))
                    link(nc.vector.memset(msk[0:64, 0, w - 64:w], NEG_MASK))
                    dve.sem_inc(sem_mask, 1)
                elif kind == "HS":
                    _, b, j = step
                    dve.wait_ge(sem_hs_pe, n + 1)
                    dve.wait_ge(sem_sel_pe, n)
                    nc.vector.tensor_scalar(r_s.rearrange("p (a n) -> p a n", a=2), ps[:, 4:6, 0:HALF_S], 0.0,
                                            wicol[:, j, b:b + 1], ALU.max, ALU.mult).then_inc(sem_hs_r, 1)
                elif kind == "ISCS":
                    dve.wait_ge(sem_sel_pe, 2 * NB)
                    nc.vector.memset(isc[:, KEYS_S:KEYS_S + PAD_S], 3.0e38)
                    nc.vector.tensor_copy(isc[:, 0:KEYS_S].rearrange("p (a n) -> p a n", a=2), ps[:, 6:8, 0:HALF_S]
                                          ).then_inc(sem_iscs, 1)

            def divide(b, h, n):
                dve.wait_ge(sem_s_exp, n + 1)
                link(nc.vector.reciprocal(rs[:, h:h + 1], sm[:, h:h + 1]))
                p = p_all[:, h, 0:P * (b + 1)]
                nc.vector.tensor_scalar(p, p, rs[:, h:h + 1], None, ALU.mult).then_inc(sem_s_norm, 1)

            def softmax_step(step):
                kind, n = step[0], NTH[step]
                if kind == "KK":
                    w = 512 if step[1] == "A" else 1024
                    dve.wait_ge(sem_kk_hi, n + 1)
                    low(keys_lo[:, 0:w], raw[:, 0:w], keys_hi[:, 0:w]).then_inc(sem_kk_lo, 1)
                elif kind == "VV":
                    w = 512 if step[1] == "A" else 1024
                    dve.wait_ge(sem_vv_hi, n + 1)
                    low(v_lo[:, 0:w], raw[:, 0:w], v_hi[:, 0:w]).then_inc(sem_vv_lo, 1)
                elif kind == "QQ":
                    u = n % 2
                    dve.wait_ge(sem_qq_hi, n + 1)
                    low(q_lo[:, u], qraw[:, 512 * u:512 * u + 512], q_hi[:, u]).then_inc(sem_qq_lo, 1)
                elif kind == "S":
                    _, b, kv, h = step
                    dve.wait_ge(sem_s_pe, n + 1)
                    if h == 0:
                        dve.wait_ge(sem_pt_pe, before(step, "PT"))
                        dve.wait_ge(sem_x_read, 9)
                        dve.wait_ge(sem_pvs_pe, before(step, "VS"))
                    v, like = score_view(4 + 2 * (h % 2), b)
                    nc.vector.tensor_tensor_reduce(out=like(p_all[:, h]), in0=v, in1=like(msk[:, NTH["QQ", b, kv] % 2]),
                                                   scale=1.0, scalar=-3.0e38, op0=ALU.add, op1=ALU.max,
                                                   accum_out=mx[:, h:h + 1]).then_inc(sem_s_max, 1)
                    dve.wait_ge(sem_s_max, n + 1)
                    nc.vector.tensor_scalar(nb_[:, h:h + 1], mx[:, h:h + 1], -SCALE, None, ALU.mult
                                            ).then_inc(sem_s_nb, 1)
                    if h > 0:
                        divide(b, h - 1, n - 1)
                elif kind == "NRM":
                    _, b, kv = step
                    divide(b, 3, NTH["S", b, kv, 3])
                elif kind == "PT":
                    dve.wait_ge(sem_pt_hi, n + 1)
                    low(pt_lo[:, n % 2], ps[:, 6 + n % 2], pt_hi[:, n % 2]).then_inc(sem_pt_lo, 1)
                elif kind == "ZZ":
                    dve.wait_ge(sem_pv_pe, before(step, "PT"))
                    dve.wait_ge(sem_z_out, 16 * n)
                    nc.vector.tensor_tensor(zat[:], ps[:, 4], sga[:, n % 2], ALU.mult).then_inc(sem_z_dve, 1)
                elif kind == "SS":
                    b = step[1]
                    dve.wait_ge(sem_ss_pe, b + 1)
                    dve.wait_ge(sem_ksm_ld[b % 2], 16 * 8 * (b // 2 + 1))
                    dve.wait_ge(sem_ps_tr, b)
                    dve.wait_ge(sem_pt_pe, PT_A)
                    m = msk[:, b % 2, 0:KEYS_S].rearrange("p (a n) -> p a n", a=2)
                    nc.vector.tensor_tensor_reduce(out=p_s.rearrange("p (a n) -> p a n", a=2), in0=ps[:, 6:8, 0:HALF_S],
                                                   in1=m, scale=1.0, scalar=-3.0e38, op0=ALU.add, op1=ALU.max,
                                                   accum_out=mx_s).then_inc(sem_ss_max, 1)
                    dve.wait_ge(sem_ss_max, n + 1)
                    nc.vector.tensor_scalar(nb_s, mx_s, -SCALE, None, ALU.mult).then_inc(sem_ss_nb, 1)
                    dve.wait_ge(sem_ss_exp, n + 1)
                    link(nc.vector.reciprocal(rs_s, sm_s))
                    nc.vector.tensor_scalar(p_s, p_s, rs_s, None, ALU.mult).then_inc(sem_ss_norm, 1)
                elif kind == "VS":
                    b = step[1]
                    dve.wait_ge(sem_pvs_pe, b + 1)
                    g = z_s[:, :, NS * b:NS * b + NS]
                    nc.vector.tensor_tensor(g, ps[:, 6, 0:P].rearrange("p (h q) -> p h q", h=8), g, ALU.mult
                                            ).then_inc(sem_vs_dve, 1)

            def final_step(step):
                kind, n = step[0], NTH[step]
                if kind == "RMS":
                    k = TT[step[1]]
                    dve.wait_ge(sem_nat_sq, KT * (n + 1))
                    dve.wait_ge(sem_fin, 10 * n)
                    link(nc.vector.tensor_reduce(o_stat[0][:, 0:k], o_ssq[:, 0:k, :], AX_X, ALU.add))
                    nc.vector.tensor_scalar(o_stat[1], o_stat[0], 1.0 / D, EPS, ALU.mult, ALU.add).then_inc(sem_o_ms, 1)
                    dve.wait_ge(sem_o_rt, n + 1)
                    link(inverse_root(o_stat))
                elif kind == "FIN":
                    i = step[1]
                    dve.wait_ge(sem_fx_ld[final_slot(i)], FIN_LOADS[i])
                    o, r = (fin_o[:, i % 2], i) if i < 5 else (o_nat[:, i - 5], i - 5)
                    for c in range(2):
                        cut = slice(D // 2 * c, D // 2 * (c + 1))
                        nc.vector.scalar_tensor_tensor(out=o[:, cut], in0=o[:, cut], scalar=o_stat[3][:, r:r + 1],
                                                       in1=residual(i)[:, cut], op0=ALU.mult, op1=ALU.add
                                                       ).then_inc(sem_fin, 1)

            nc.vector.memset(o_stat[0], 0.0)
            for i in range(6):
                if i < 5:
                    normalise_x(i)
                if i > 0:
                    for m in range(4 * (i - 1), 4 * i):
                        unit_low(m)
            for slot in range(TAIL + SLOTS):
                n, s = divmod(slot, SLOTS)
                if n and s == 0 and TILES[n - 1][1] == "hc":
                    conv_input(n - 1)
                if n and s == 0 and TILES[n - 1][1] == "bg":
                    conv_taps(n - 1)
                if n and s == 1 and TILES[n - 1][1] == "gb":
                    conv_gate(n - 1)
                if n and s == 2 and TILES[n - 1][1] in TURNED:
                    turned_out(n - 1)
                if n == NP - 1 and s % 2:
                    for i in range(4):
                        unit_low(NX_A + 2 * (s - 1) + i)
                for g in range(2):
                    if n == PHASE_LAST[1 + g]:
                        z_low(g, 2 * s)
                        z_low(g, 2 * s + 1)
                if slot < TAIL:
                    for step in SIDE.get(slot, ()):
                        index_step(step)
                        softmax_step(step)
                        final_step(step)
                        if step[0] == "NX":
                            normalise_x(step[1])
            for step in SIDE[TAIL]:
                final_step(step)


FIN_LOADS = [32 * (i // 2 + 1) if i < 5 else 16 for i in range(9)]


def final_slot(i):
    return i % 2 if i < 5 else i - 3


_INS = ["x_prompt", "x_sample", "cache_k", "cache_v", "cache_idx_k", "state_conv", "g_pre", "w_in", "w_conv",
        "w_out", "g_post"]
_OUTS = [(1, 1024, 2048), (8, 16, 2048), (1, 1, 1024, 2, 128), (1, 1, 1024, 2, 128), (1, 1, 1024, 64),
         (1, 1, 2, 1024), (1, 8, 16, 2, 128), (1, 8, 16, 2, 128), (1, 8, 16, 64), (1, 8, 2, 1024)]


def kernel(**inputs):
    import numpy as np
    import concourse.bacc as bacc
    from concourse.bass_utils import run_bass_kernel_spmd

    nc = bacc.Bacc("TRN2", target_bir_lowering=False, num_devices=1, dynamic_dma_scratch_size=1024)
    arrays, args = {}, []
    for name in _INS:
        a = np.ascontiguousarray(inputs[name])
        arrays["in_" + name] = a
        args.append(nc.dram_tensor("in_" + name, a.shape, mybir.dt.from_np(a.dtype), kind="ExternalInput").ap())
    for i, shape in enumerate(_OUTS):
        args.append(nc.dram_tensor(f"out_{i}", shape, F32, kind="ExternalOutput").ap())
    build(nc, *args)
    r = run_bass_kernel_spmd(nc, [arrays], core_ids=[0])
    return tuple(r.results[0][f"out_{i}"] for i in range(len(_OUTS)))
```

```python
from contextlib import ExitStack

import concourse.bass as bass
from concourse import mybir

F32 = mybir.dt.float32
F32R = mybir.dt.float32r
BF16 = mybir.dt.bfloat16
ALU = mybir.AluOpType
ACT = mybir.ActivationFunctionType
AX_X = mybir.AxisListType.X

P = 128
D = 2048
KT = D // P
SEQ, NB, NS = 1024, 8, 16
PAST = 512
T_A, T_B = 512 + NB * NS, 512
T_ALL = T_A + T_B
TOKENS = {"A": T_A, "B": T_B}
COLUMN = {"A": 0, "B": T_A}
TT = {"A": T_A // P, "B": T_B // P}
HD, IH, ID = 128, 16, 64
TOPK = 256
KEYS_S = PAST + NS
HALF_S = KEYS_S // 2
TOPK_S = min(TOPK, KEYS_S // 4)
PAD_S = -TOPK_S % 8
ROUNDS, ROUNDS_S = TOPK // 8, (TOPK_S + PAD_S) // 8
SCALE = HD ** -0.5
EPS = 1e-6
NEG_MASK = -1e30
NEG_LATER = -3.0e38
NEG_TAKEN = -3.4e38
NEG_CUT = -3.3e38

Q0, K0, V0, GA0, QI0, KI0 = 0, 1024, 1280, 1536, 2560, 3584
BG0, CG0, HC0, GB0 = 3664, 4688, 5712, 6736

_FIRST = ([("kiwi", 0, KI0)] + [("k", i, K0 + P * i) for i in range(2)] + [("v", i, V0 + P * i) for i in range(2)]
          + [("qi", i, QI0 + P * i) for i in range(8)] + [("q", i, Q0 + P * i) for i in range(8)])
_CONV = [t for c in range(8) for t in (("cg", c, CG0 + P * c), ("hc", c, HC0 + P * c),
                                       ("bg", c, BG0 + P * c), ("gb", c, GB0 + P * c))]
_GATE = [("ga", i, GA0 + P * i) for i in range(8)]
PROJ = {"A": _FIRST + _CONV + _GATE, "B": _FIRST + _GATE[:6] + _CONV + _GATE[6:]}
OUTP = [("o", i, 2 * P * (i // 2)) for i in range(KT)]
OW, PAIRS = 2 * P, KT // 2
NP, NO = len(PROJ["A"]), len(OUTP)
TILES = ([("A", *t) for t in PROJ["A"]] + [("B", *t) for t in PROJ["B"]]
         + [("A", *t) for t in OUTP] + [("B", *t) for t in OUTP])
NT = len(TILES)
OUT_A, OUT_B = 2 * NP, 2 * NP + NO
PHASE_LAST = (NP - 1, OUT_A - 1, OUT_B - 1, NT - 1)
SLOTS = 8
PER = KT // SLOTS
RING = 3
TURNED = ("kiwi", "k", "v")
SPILLED = ("kiwi", "k", "qi", "q", "ga", "gb")
BUFFERED = SPILLED + ("v",)


def tile_number(group, kind, index):
    return next(n for n, t in enumerate(TILES) if t[:3] == (group, kind, index))


EV = {}
EV_SPILLS = {}
TURN = {}
_c = [0, 0]
for _i, _t in enumerate(TILES):
    if _t[1] in BUFFERED:
        EV[_i] = len(EV)
        _c[EV[_i] % 2] += _t[1] in SPILLED
        EV_SPILLS[_i] = tuple(_c)
    if _t[1] in TURNED:
        TURN[_i] = len(TURN)
EV_TILE = {v: k for k, v in EV.items()}


def turned_before(n, group=None, kinds=TURNED):
    return sum(1 for x in TURN if x < n and TILES[x][1] in kinds and group in (None, TILES[x][0]))


def block_column(b):
    return P * b + (P if b >= 4 else 0)


def z_pieces(slot):
    n, s = divmod(slot, SLOTS)
    if n == PHASE_LAST[1]:
        return [(0, 2 * s), (0, 2 * s + 1)]
    if n == PHASE_LAST[2]:
        return [(1, 2 * s), (1, 2 * s + 1)] if s < 4 else [(1, 4 + s)]
    return [(1, 12 + s)] if n == PHASE_LAST[2] + 1 and s < 4 else []


def mask_half(b):
    return int(b != "s" and b >= 4)


def group_of(b):
    return "A" if b < 4 else "B"


def pieces(b):
    n = P * (b + 1)
    k = 1 if n <= 512 else 2
    return k, n // k


US_A, US_B = 1.63, 1.30
W = dict(top=1.13, head=1.15, first=1.5, keys=3, s=0.5, norm=1, pt=1.4, zz=1.5, hs=2.5, iks=2.5, sa=1.0, sb=1.2,
         streams=0.9, ks=2.25, ss=1.5, ps=1.25, start=1.5)


def index_steps(b, us):
    n = P * (b + 1)
    out = [(("QI", b, 0), 1)]
    for hp in range(IH // 2):
        out += [(("HEAD", b, hp), (2 * (n + 60) / 960 * W["head"] + 0.3) / us)]
        if hp == 2:
            out += [(("QI", b, 1), 0)]
    out[-1] = (out[-1][0], out[-1][1] + W["first"] / us)
    return out + [(("TK", b, r), W["top"] * 2 * 2 * (n + 190) / 960 / us) for r in range(0, ROUNDS, 2)]


def stream_index_steps():
    out = [(("QS",), 2)]
    for b in range(NB):
        out += [(("IKS", b), W["iks"]), (("HS", b, 0), 1.5), (("HS", b, 1), W["hs"]), (("SEL", b), 0)]
    return out + [(("ISCS",), 1)] + [(("TK", "s", r), 2) for r in range(0, ROUNDS_S, 2)]


def softmax_steps(group, us):
    out = []
    blocks = range(4) if group == "A" else range(4, 8)
    units = [(b, kv) for kv in range(2) for b in blocks]
    for i, (b, kv) in enumerate(units):
        if i == 0:
            out += [(("KK", group, 0), 2), (("QQ", *units[0]), 2)]
        if b == blocks[0]:
            out += [(("VV", group, kv), 1)]
        n = P * (b + 1)
        out += [(("S", b, kv, h), ((n + 60) / 960 + n / 1920 + W["s"]) / us) for h in range(4)]
        out += [(("NRM", b, kv), (W["norm"] + n / 1000) / us), (("PT", b, kv, 0), W["pt"] / us)]
        if i + 1 < len(units):
            if b == blocks[-1]:
                out += [(("KK", group, 1), 0)]
            out += [(("QQ", *units[i + 1]), 0)]
        out += [(("PT", b, kv, j), W["pt"] / us) for j in range(1, b + 1)]
        out += [(("ZZ", b, kv), W["zz"] / us)]
    return out


def stream_softmax_steps():
    out = [(("QQS",), 1), (("KS", 0), 3)]
    for b in range(NB):
        out += [(("SS", b), W["ss"])] + ([(("KS", b + 1), W["ks"])] if b + 1 < NB else [])
        out += [(("PS", b), W["ps"]), (("VS", b), 1)]
    return out + [(("ZS",), 1)]


def wider(steps, factor):
    return [(step, factor * width) for step, width in steps]


def timetable():
    side, placed = {}, [0.0]

    def place(steps, tile, end):
        at = max(float(SLOTS * tile), placed[0])
        for step, width in steps:
            side.setdefault(min(int(at), SLOTS * end - 1), []).append(step)
            at += width
        placed[0] = at

    place([(("CHUNKS", 0), 1), (("CHUNKS", 1), 1), (("IK", "A"), 2)]
          + index_steps(2, US_A) + index_steps(3, US_A) + stream_index_steps(), 22, NP - 7)
    place([(("NX", i), 8) for i in range(5, 9)], NP - 6, NP - 1)
    place(wider(softmax_steps("A", US_B), W["sa"]) + wider(stream_softmax_steps(), W["streams"]),
          NP + W["start"], NP + 22)
    softmax_b = wider(softmax_steps("B", US_A), W["sb"])
    first, softmax_b = softmax_b[:3], softmax_b[3:]
    cut = [step for step, _ in softmax_b].index(("ZZ", 7, 0)) + 1
    second = (("KK", "B", 1), ("QQ", 4, 1))
    last_block = index_steps(7, US_B)
    place([(("IK", "B"), W["keys"])] + [s for b in range(4, 7) for s in index_steps(b, US_B)]
          + last_block[:12] + wider(first, 0) + last_block[12:]
          + [s for s in softmax_b[:cut] if s[0] not in second], NP + 17, 2 * NP + 3)
    place([(step, 2) for step in second] + softmax_b[cut:], 2 * NP + 1.7, OUT_B - 1)
    place([(("RMS", "A"), 3)] + [(("FIN", i), 16) for i in range(5)], OUT_B + 1, OUT_B + 14)
    side[TAIL] = [("RMS", "B")] + [("FIN", i) for i in range(5, 9)]
    return side


TAIL = SLOTS * NT
SIDE = timetable()
ORDER = [s for slot in sorted(SIDE) for s in SIDE[slot]]
NTH = {}
for _s in ORDER:
    NTH[_s] = sum(1 for x in NTH if x[0] == _s[0])
POSITION = {s: i for i, s in enumerate(ORDER)}


def before(step, kind):
    return sum(1 for s in ORDER[:POSITION[step]] if s[0] == kind)


AHEAD = 10
SLOT_OF = {s: slot for slot in SIDE for s in SIDE[slot]}
LOADING = ("IK", "QI", "QS", "IKS", "KK", "VV", "QQ", "QQS", "KS", "SS", "NX", "FIN")


def released_by(step):
    kind, n = step[0], NTH[step]
    same = [s for s in ORDER if s[0] == kind]
    before_it = ORDER[:POSITION[step]]
    if kind in ("KS", "QI") and n > 0:
        return same[n - 1]
    if kind == "KK" and n > 0:
        return [s for s in ORDER if s[0] == "VV"][n - 1]
    if kind == "VV":
        return [s for s in ORDER if s[0] == "KK"][n]
    if kind == "QQ" and n == 8:
        return [s for s in before_it if s[0] == "QI"][-1]
    if kind == "QQ":
        return max([s for s in before_it if s[0] == "TK"][-1:]
                   + [s for s in ORDER if s[0] == "ZZ"][max(n - 2, 0):max(n - 1, 0)], key=POSITION.get)
    if kind in ("IKS", "FIN") and n > 1:
        return same[n - 2]
    if kind == "SS":
        return [s for s in before_it if s[0] in ("VS", "ZZ")][-1]
    if kind == "QQS":
        return [s for s in before_it if s[0] in ("QQ", "VV")][-1]
    if step == ("IK", "B"):
        return ("ZS",)
    return None


def spilled_at(step):
    kind = step[0]
    source = {"IK": ("kiwi", 0), "QI": ("qi", 7), "QS": ("qi", 7), "KK": ("k", 1), "VV": ("v", 1),
              "QQ": ("ga", 3 + 4 * (step[-1] == 1)),
              "QQS": ("ga", 7), "FIN": ("o", KT - 1)}.get(kind)
    if source is None:
        return 0
    group = step[1] if kind in ("IK", "KK", "VV") else group_of(step[1]) if kind in ("QI", "QQ") else "A"
    return SLOTS * (tile_number(group, *source) + 1) + 5


LOADS = {}
for _s in ORDER:
    if _s[0] in LOADING and SLOT_OF[_s] < TAIL:
        _free = released_by(_s)
        _at = SLOT_OF[_free] + (_free[0] in ("TK", "ZS")) if _free else 0
        LOADS.setdefault(max(SLOT_OF[_s] - AHEAD, _at, spilled_at(_s)), []).append(_s)


def last_rounds(step):
    return step[2] + 2 >= (ROUNDS_S if step[1] == "s" else ROUNDS)


MASKS = [s[1] for s in ORDER if s[0] == "CHUNKS" or (s[0] == "TK" and last_rounds(s))]
MASKS_A = sum(1 for b in MASKS if b == "s" or b < 4)
UNITS_A = sum(1 for s in ORDER if s[0] == "ZZ" and s[1] < 4)
UNITS = sum(1 for s in ORDER if s[0] == "ZZ")
HEADS_A = 2 * sum(1 for s in ORDER if s[0] == "HEAD" and s[1] < 4)
HEADS = 2 * sum(1 for s in ORDER if s[0] == "HEAD")
QI_A = sum(1 for s in ORDER if s[0] == "QI" and s[1] < 4)
QI_ALL = sum(1 for s in ORDER if s[0] == "QI")
PT_A = sum(1 for s in ORDER if s[0] == "PT" and s[1] < 4)

UNITS_X = [(i, j) for i in range(5) for j in range(4)] + [(5 + i, j) for j in range(4) for i in range(4)]
NX_A, NX_B = 20, 16


def build(nc, x_prompt, x_sample, cache_k, cache_v, cache_idx_k, state_conv, g_pre, w_in, w_conv, w_out, g_post,
          y_prompt, y_sample, new_k_p, new_v_p, new_ik_p, conv_p, new_k_s, new_v_s, new_ik_s, conv_s):
    def scratch(name, rows, cols=T_ALL, dt=F32):
        return nc.dram_tensor(name, (rows, cols), dt).ap()

    z_q, z_k, z_kiwi, z_qi = scratch("z_q", 1024), scratch("z_k", 256), scratch("z_kiwi", P), scratch("z_qi", 1024)
    z_ga, z_mix = scratch("z_ga", 1024), scratch("z_mix", D)
    z_mask = scratch("z_mask", 9 * P, SEQ, BF16)
    z_og = scratch("z_og", T_A, D)
    spill_to = {"q": z_q, "k": z_k, "kiwi": z_kiwi, "qi": z_qi, "ga": z_ga, "gb": z_mix[1024:D]}

    w_in_v = w_in[0].rearrange("(k p) e -> p k e", p=P)
    w_out_v = w_out[0].rearrange("(k p) e -> p k e", p=P)
    xs = x_sample.rearrange("b t d -> (b t) d")
    ys = y_sample.rearrange("b t d -> (b t) d")

    def token_rows(prompt, streams, i):
        if i == 4:
            return streams
        r = P * (i if i < 4 else i - 1)
        return prompt[r:r + P]

    with ExitStack() as ctx:
        def semaphores(names):
            return tuple(ctx.enter_context(nc.semaphore(name)) for name in names.split())

        def semaphore_ring(name, k):
            return [ctx.enter_context(nc.semaphore(f"{name}{i}")) for i in range(k)]

        (sem_w_hi, sem_w_lo, sem_gemm, sem_passed, sem_nat_pe, sem_nat_cp, sem_nat_sq, sem_o_cp, sem_og_out,
         sem_cg_rdy, sem_hc_rdy,
         sem_gb_silu, sem_gb_used, sem_const, sem_wcv_ld, sem_st_ld, sem_g_ld) = semaphores(
            "w_hi w_lo gemm passed nat_pe nat_cp nat_sq o_cp og_out "
            "cg_rdy hc_rdy gb_silu gb_used const wcv_ld st_ld g_ld")
        (sem_x_ssq, sem_x_ms, sem_x_rt, sem_x_rs, sem_x_sc, sem_x_rdy, sem_x_half, sem_x_read, sem_x_tr, sem_x_hi,
         sem_x_lo, sem_cs_out, sem_z_hi,
         sem_z_lo) = semaphores(
            "x_ssq x_ms x_rt x_rs x_sc x_rdy x_half x_read x_tr x_hi x_lo cs_out z_hi z_lo")
        (sem_ik_ld, sem_ik_hi, sem_ik_lo, sem_qi_ld, sem_qi_hi, sem_qi_lo, sem_head_pe, sem_relu, sem_isum, sem_mask,
         sem_mask_out) = semaphores(
            "ik_ld ik_hi ik_lo qi_ld qi_hi qi_lo head_pe relu isum mask mask_out")
        (sem_qs_ld, sem_iks_tr, sem_iks_cp, sem_hs_pe, sem_hs_relu, sem_hs_r, sem_sel_pe, sem_iscs) = semaphores(
            "qs_ld iks_tr iks_cp hs_pe hs_relu hs_r sel_pe iscs")
        (sem_kk_ld, sem_kk_hi, sem_kk_lo, sem_vv_ld, sem_vv_hi, sem_vv_lo, sem_qq_hi, sem_qq_lo, sem_s_pe, sem_s_max,
         sem_s_nb, sem_s_exp, sem_s_norm, sem_pt_pe, sem_pt_hi, sem_pt_lo, sem_pv_pe, sem_z_dve) = semaphores(
            "kk_ld kk_hi kk_lo vv_ld vv_hi vv_lo qq_hi qq_lo s_pe s_max s_nb s_exp s_norm pt_pe pt_hi pt_lo pv_pe "
            "z_dve")
        (sem_z_out, sem_qqs_ld, sem_ks_tr, sem_ks_cp, sem_ss_pe, sem_ss_max, sem_ss_nb, sem_ss_exp, sem_ss_norm,
         sem_ps_tr, sem_ps_cp, sem_pvs_pe, sem_vs_dve, sem_zs_out) = semaphores(
            "z_out qqs_ld ks_tr ks_cp ss_pe ss_max ss_nb ss_exp ss_norm ps_tr ps_cp pvs_pe vs_dve zs_out")
        (sem_o_ms, sem_o_rt, sem_fin, sem_fin_out, sem_dve_chain, sem_pool_chain) = semaphores(
            "o_ms o_rt fin fin_out dve_chain pool_chain")
        sem_w_ld = semaphore_ring("w_ld", RING)
        sem_evac = semaphore_ring("evac", 2)
        sem_ev_rdy = semaphore_ring("ev_rdy", 2)
        sem_ev_out = semaphore_ring("ev_out", 2)
        sem_nat_out = semaphore_ring("nat_out", 2)
        sem_x_ld = semaphore_ring("x_ld", 8)
        sem_z_ld = semaphore_ring("z_ld", 5)
        sem_qq_ld = semaphore_ring("qq_ld", 2)
        sem_iks_ld = semaphore_ring("iks_ld", 2)
        sem_ksk_ld = semaphore_ring("ksk_ld", 2)
        sem_ksv_ld = semaphore_ring("ksv_ld", 1)
        sem_ksm_ld = semaphore_ring("ksm_ld", 2)
        sem_fx_ld = semaphore_ring("fx_ld", 6)

        def sb(name, shape, dt=F32, stack=ctx):
            return stack.enter_context(nc.sbuf_tensor(name, shape, dt))

        act_hi = sb("act_hi", [P, KT, T_A], F32R)
        act_lo = sb("act_lo", [P, KT, T_A], F32R)
        w_raw = sb("w_raw", [P, RING, KT // 2, P])
        w_hi = sb("w_hi", [P, RING, KT // 2, P], F32R)
        w_lo = sb("w_lo", [P, RING, KT // 2, P], F32R)
        ev = sb("ev", [P, 2, T_A])
        o_stage = ev[:].rearrange("p u t -> p (u t)").rearrange("p (i d) -> p i d", d=OW)
        conv = sb("conv", [P, 3072])
        c_cg, c_y, c_g = conv[:, 0:T_A], conv[:, T_A:2 * T_A], conv[:, 2 * T_A:3 * T_A]
        c_up = conv[:, 1920:1920 + 514]
        c_us = conv[:, 2440:2440 + NB * 18].rearrange("p (b t) -> p b t", b=NB)

        def z_place(g, k):
            ring, t = (4, 5)[g], (T_A, T_B)[g]
            r = k % ring
            return conv[:, t * r:t * (r + 1)], sem_z_ld[r], 16 * (k // ring + 1 + (KT // 4 if g and r < 4 else 0))

        x_junk = [conv[:, 2048 + 512 * i:2560 + 512 * i].bitcast(BF16) for i in range(2)]
        nat = sb("nat", [P, 5, P])
        o_junk = [nat[:, i].bitcast(BF16) for i in range(5)]
        gbc = sb("gbc", [P, D])
        wi_nat = sb("wi_nat", [P, 9, IH])
        wicol = sb("wicol", [P, 2, NB])
        ident = sb("ident", [P, P])
        sel = sb("sel", [P, 112 + P])
        wcv = sb("wcv", [P, 3, 8])
        st = sb("st", [P, 8, 2 * NB])
        cs = sb("cs", [P, 8, 2 + 2 * NB])
        u_prev = sb("u_prev", [P, 8, 2])
        top8 = sb("top8", [P, 8])
        o_ssq = sb("o_ssq", [P, 5, PAIRS])
        stat = sb("stat", [P, 64])
        mx, nb_, sm, rs = (stat[:, 4 * i:4 * i + 4] for i in range(4))
        mx_s, nb_s, sm_s, rs_s = (stat[:, 16 + i:17 + i] for i in range(4))
        x_stat = [[stat[:, 44 + 6 * u + i:45 + 6 * u + i] for i in range(4)] for u in range(2)]
        x_sums = [stat[:, 48 + 6 * u:50 + 6 * u] for u in range(2)]
        o_stat = [stat[:, 24 + 5 * i:29 + 5 * i] for i in range(4)]

        attention = ExitStack()
        F = sb("F", [P, 4096], F32, attention)
        raw = sb("raw", [P, 1024], F32, attention)
        qraw = sb("qraw", [P, 1024], F32, attention)
        keys_hi = sb("keys_hi", [P, 1024], F32R, attention)
        keys_lo = sb("keys_lo", [P, 1024], F32R, attention)
        qv = sb("qv", [P, 2048], F32R, attention)
        qst = qv[:].rearrange("p (h t) -> p h t", h=IH)
        v_hi, v_lo = qv[:, 0:1024], qv[:, 1024:2048]
        isc = sb("isc", [P, 1032], F32, attention)
        msk = sb("msk", [P, 2, 1024], BF16, attention)
        q_hi = sb("q_hi", [P, 2, 512], F32R, attention)
        q_lo = sb("q_lo", [P, 2, 512], F32R, attention)
        pt_hi = sb("pt_hi", [P, 2, 512], F32R, attention)
        pt_lo = sb("pt_lo", [P, 2, 512], F32R, attention)
        sga = sb("sga", [P, 2, 512], F32, attention)
        zat = sb("zat", [P, 512], F32, attention)
        xh = [(F[:, 0:1024], F[:, 1024:2048]), (F[:, 2048:3072], F[:, 3072:4096]),
              (conv[:, 0:1024], conv[:, 1024:2048]), (raw[:], qraw[:])]
        qs_v = F[0:ID, 0:2048].rearrange("p (b h q) -> p b h q", b=NB, h=IH)
        iknat = F[:, 2048:2560].rearrange("p (s t d) -> p s t d", s=2, t=4)
        ikt, r_s = F[0:ID, 2560:2560 + KEYS_S], F[:, 3088:3088 + KEYS_S]
        ik_new = F[0:ID, 3616:3616 + P]
        knat = F[:, :].rearrange("p (t x) -> p t x", t=4)[:, :, 512:768]
        kts = F[:, 768:768 + 2048].rearrange("p (k x) -> p k x", k=2)[:, :, 0:KEYS_S]
        p_s, vs_new = F[:, 2816:2816 + KEYS_S], F[0:NS, 3840:4096]
        vs = sga[:].rearrange("p u (t e) -> p (u t) e", t=2)
        pts = isc[:, 0:640].rearrange("p (t n) -> p t n", t=5)
        k_new = isc[:, 640:896].rearrange("p (k t) -> p k t", k=2)
        z_s = raw[:].rearrange("p (h t) -> p h t", h=8)
        p_all = F[:, :].rearrange("p (h s) -> p h s", h=4)
        attention.close()
        o_nat = sb("o_nat", [P, 4, D])
        fin_o = sb("fin_o", [P, 2, D])
        fin_x = sb("fin_x", [P, 2, D])

        ps = ctx.enter_context(nc.psum_tensor("ps", [P, 8, 512], F32))
        block = ctx.enter_context(nc.Block())

        def out_weights(w, h):
            return w[:, h % RING].rearrange("p k e -> p (k e)").rearrange("p (k e) -> p k e", e=OW)

        def bank_use(pair, i):
            return (3 * pair if pair < PAIRS else 3 * PAIRS + 2 * (pair - PAIRS)) + i // 2

        def out_place(pair, i):
            return ps[:, bank_use(pair, i) % 4, OW * (i % 2):OW * (i % 2 + 1)]

        def tile_view(n):
            a = 2 * (n % 2)
            if TILES[n][0] == "A":
                return ps[:, a:a + 2, 0:T_A // 2], lambda t: t[:, 0:T_A].rearrange("p (a n) -> p a n", a=2)
            return ps[:, a, 0:T_B], lambda t: t[:, 0:T_B]

        def score_view(bank, b):
            k, c = pieces(b)
            return ps[:, bank:bank + k, 0:c], lambda t: t[:, 0:k * c].rearrange("p (a n) -> p a n", a=k)

        def residual(i):
            return (fin_x if i < 7 else fin_o)[:, i % 2]

        def ev_free(e):
            old = EV_TILE[e - 2]
            return 16 * EV_SPILLS[old][e % 2], turned_before(old + 1)

        @block.sync
        def _(sp):
            def spilled(group, kind, index):
                done = EV_SPILLS[tile_number(group, kind, index)]
                sp.wait_ge(sem_ev_out[0], 16 * done[0])
                sp.wait_ge(sem_ev_out[1], 16 * done[1])

            def load_weights(h):
                if h < 2 * NT:
                    sp.wait_ge(sem_w_lo, max(h - RING + 1, 0))
                    _, kind, _, col = TILES[h // 2]
                    dst, src = w_raw[:, h % RING], w_in_v[:, KT // 2 * (h % 2):KT // 2 * (h % 2 + 1), col:col + P]
                    if kind == "o":
                        q = h % 4
                        dst, src = out_weights(w_raw, h), w_out_v[:, KT // 4 * q:KT // 4 * (q + 1), col:col + OW]
                    sp.dma_start(dst, src).then_inc(sem_w_ld[h % RING], 16)

            def load_x(i):
                buf = xh[i % 5 % 4] if i < 5 else xh[i - 5]
                slot = i % 5 % 4 if i < 5 else i - 5
                if i == 4:
                    sp.wait_ge(sem_x_read, 1)
                if i in (5, 6):
                    sp.wait_ge(sem_sel_pe, NB)
                if i == 7:
                    sp.wait_ge(sem_gb_used, 8)
                if i == 8:
                    sp.wait_ge(sem_ik_lo, 1)
                    sp.wait_ge(sem_qi_lo, QI_A)
                rows = token_rows(x_prompt[0], xs, i)
                for c in range(2):
                    sp.dma_start(buf[c], rows[:, 1024 * c:1024 * (c + 1)]).then_inc(sem_x_ld[2 * slot + c], 16)

            def load_z(g, k):
                m = k + KT * g
                group = "AB"[g]
                if k == 0:
                    sp.wait_ge(sem_z_out, 16 * (UNITS_A, UNITS)[g])
                    sp.wait_ge(sem_zs_out, 16)
                    spilled(group, "gb", 7)
                    sp.wait_ge(sem_gb_used, 16)
                sp.wait_ge(sem_z_lo, KT * g + max(k - (3, 4)[g], 0))
                place, loaded, _ = z_place(g, k)
                sp.dma_start(place,
                             z_mix[P * k:P * (k + 1), COLUMN[group]:COLUMN[group] + TOKENS[group]]
                             ).then_inc(loaded, 16)

            def spill(n):
                group, kind, index, _ = TILES[n]
                e, t, c = EV[n], TOKENS[group], COLUMN[group]
                sp.wait_ge(sem_ev_rdy[e % 2], e // 2 + 1)
                sp.dma_start(spill_to[kind][P * index:P * (index + 1), c:c + t], ev[:, e % 2, 0:t]
                             ).then_inc(sem_ev_out[e % 2], 16)

            def store_turned(n):
                group, kind, index, _ = TILES[n]
                sp.wait_ge(sem_nat_cp, TURN[n] + 1)
                rows = slice(0, 512) if group == "A" else slice(512, 1024)
                dst_p, dst_s, w = {"kiwi": (new_ik_p[0, 0], new_ik_s[0], ID),
                                   "k": (new_k_p[0, 0][:, index], new_k_s[0][:, :, index], P),
                                   "v": (new_v_p[0, 0][:, index], new_v_s[0][:, :, index], P)}[kind]
                sp.dma_start(dst_p[rows].rearrange("(i p) d -> p i d", p=P), nat[:, 0:4, 0:w]
                             ).then_inc(sem_nat_out[0], 16)
                if group == "A":
                    sp.dma_start(dst_s.rearrange("b t d -> (b t) d"), nat[:, 4, 0:w]).then_inc(sem_nat_out[1], 16)

            def store_product(n):
                c = TILES[n][3]
                sp.wait_ge(sem_o_cp, bank_use(TILES[n][2] // 2, 4) + 1)
                sp.dma_start(z_og[:, c:c + OW].rearrange("(i p) d -> p i d", p=P), o_stage).then_inc(sem_og_out, 16)

            def key_columns(z, group):
                return [z[:, 0:512]] if group == "A" else [z[:, 0:512], z[:, T_A:T_A + 512]]

            def index_loads(step):
                kind, n = step[0], NTH[step]
                if kind == "IK":
                    group = step[1]
                    spilled(group, "kiwi", 0)
                    if group == "A":
                        sp.wait_ge(sem_x_read, 5)
                    else:
                        sp.wait_ge(sem_vv_lo, 2)
                        sp.wait_ge(sem_zs_out, 16)
                    for half in range(2):
                        for c, src in enumerate(key_columns(z_kiwi[0:ID], group)):
                            sp.dma_start(raw[ID * half:ID * half + ID, 512 * c:512 * c + 512], src
                                         ).then_inc(sem_ik_ld, 16)
                elif kind == "QI":
                    _, b, half = step
                    spilled(group_of(b), "qi", 7)
                    sp.wait_ge(sem_qi_lo, n)
                    if n == 0:
                        sp.wait_ge(sem_x_read, 5)
                    if n == QI_A:
                        sp.wait_ge(sem_qq_lo, UNITS_A)
                        sp.wait_ge(sem_ss_pe, NB)
                    src = z_qi[:, block_column(b):block_column(b) + P].rearrange("(h d) t -> d h t", d=ID)
                    for r in range(2):
                        sp.dma_start(qraw[ID * r:ID * r + ID, :].rearrange("p (h t) -> p h t", h=8),
                                     src[:, 8 * half:8 * half + 8]).then_inc(sem_qi_ld, 16)
                elif kind == "QS":
                    spilled("A", "qi", 7)
                    sp.wait_ge(sem_x_read, 5)
                    for b in range(NB):
                        c = 512 + NS * b
                        sp.dma_start(qs_v[:, b], z_qi[:, c:c + NS].rearrange("(h d) q -> d h q", d=ID)
                                     ).then_inc(sem_qs_ld, 16)
                    for j in range(2):
                        for h in range(8):
                            row = ID + 8 * j + h
                            src = z_kiwi[row:row + 1, 512:T_A].rearrange("o (b q) -> (o q) b", q=NS)
                            sp.dma_start(wicol[NS * h:NS * h + NS, j], src, allow_slow_non_contiguous=True
                                         ).then_inc(sem_qs_ld, 16)
                    sp.dma_start(ik_new, z_kiwi[0:ID, 512:T_A]).then_inc(sem_qs_ld, 16)
                elif kind == "IKS":
                    b = step[1]
                    sp.wait_ge(sem_x_read, 5)
                    sp.wait_ge(sem_iks_tr, max(b - 1, 0))
                    sp.dma_start(iknat[:, b % 2], cache_idx_k[0, b].rearrange("(t p) d -> p t d", p=P)
                                 ).then_inc(sem_iks_ld[b % 2], 16)

            def softmax_loads(step):
                kind, n = step[0], NTH[step]
                if kind == "KK":
                    _, group, kv = step
                    spilled(group, "k", 1)
                    sp.wait_ge(sem_vv_lo, n)
                    sp.wait_ge(sem_ik_lo, 1 if group == "A" else 2)
                    sp.wait_ge(sem_x_read, 9)
                    for c, src in enumerate(key_columns(z_k[P * kv:P * kv + P], group)):
                        sp.dma_start(raw[:, 512 * c:512 * c + 512], src).then_inc(sem_kk_ld, 16)
                elif kind == "VV":
                    _, group, kv = step
                    nt = 4 if group == "A" else 8
                    sp.wait_ge(sem_nat_out[0], 16 * (TURN[tile_number(group, "v", 1)] + 1))
                    sp.wait_ge(sem_kk_lo, n + 1)
                    sp.dma_start(raw[:, 0:P * nt].rearrange("p (t d) -> p t d", t=nt),
                                 new_v_p[0, 0][0:P * nt, kv].rearrange("(t p) d -> p t d", p=P)
                                 ).then_inc(sem_vv_ld, 16)
                elif kind == "QQ":
                    _, b, kv = step
                    u, c, w = n % 2, block_column(b), P * (b + 1)
                    spilled(group_of(b), "ga", 3 + 4 * kv)
                    masks = MASKS_A if b < 4 else MASKS.index(4) + 1 if n == UNITS_A else len(MASKS)
                    sp.wait_ge(sem_mask_out, 16 * masks)
                    sp.wait_ge(sem_qi_lo, QI_A if b < 4 else QI_ALL)
                    sp.wait_ge(sem_x_read, 9)
                    sp.wait_ge(sem_qq_lo, max(n - 1, 0))
                    sp.wait_ge(sem_z_dve, max(n - 1, 0))
                    sp.wait_ge(sem_s_max, 4 * max(n - 1, 0))
                    if n >= UNITS_A:
                        sp.wait_ge(sem_ss_max, NB)
                        sp.wait_ge(sem_pvs_pe, NB)
                    sp.dma_start(qraw[:, 512 * u:512 * u + 512].rearrange("p (h t) -> p h t", h=4),
                                 z_q[512 * kv:512 * kv + 512, c:c + P].rearrange("(h d) t -> d h t", d=P)
                                 ).then_inc(sem_qq_ld[u], 16)
                    sp.dma_start(sga[:, u].rearrange("p (h t) -> p h t", h=4),
                                 z_ga[512 * kv:512 * kv + 512, c:c + P].rearrange("(h d) t -> d h t", d=P)
                                 ).then_inc(sem_qq_ld[u], 16)
                    sp.dma_start(msk[:, u, 0:w], z_mask[P * b:P * b + P, 0:w]).then_inc(sem_qq_ld[u], 16)
                elif kind == "QQS":
                    sp.wait_ge(sem_qq_lo, UNITS_A)
                    sp.wait_ge(sem_vv_lo, 2)
                    for b in range(NB):
                        c = 512 + NS * b
                        sp.dma_start(qraw[:, P * b:P * b + P].rearrange("p (h q) -> p h q", h=8),
                                     z_q[:, c:c + NS].rearrange("(h d) q -> d h q", d=P)).then_inc(sem_qqs_ld, 16)
                    sp.dma_start(z_s, z_ga[:, 512:T_A].rearrange("(h d) t -> d h t", d=P)).then_inc(sem_qqs_ld, 16)
                    sp.dma_start(k_new, z_k[:, 512:T_A].rearrange("(k d) t -> d k t", d=P)).then_inc(sem_qqs_ld, 16)
                elif kind == "KS":
                    b = step[1]
                    sp.wait_ge(sem_x_read, 9)
                    sp.wait_ge(sem_ks_tr, b)
                    sp.dma_start(knat, cache_k[0, b].rearrange("(t p) k d -> p t (k d)", p=P)
                                 ).then_inc(sem_ksk_ld[b % 2], 16)
                    sp.wait_ge(sem_s_max, 4 * UNITS_A)
                    sp.wait_ge(sem_ss_max, max(b - 1, 0))
                    for h in range(8):
                        sp.dma_start(msk[NS * h:NS * h + NS, b % 2, 0:KEYS_S],
                                     z_mask[8 * P + NS * b:8 * P + NS * (b + 1), 0:KEYS_S]
                                     ).then_inc(sem_ksm_ld[b % 2], 16)
                elif kind == "SS":
                    b = step[1]
                    sp.wait_ge(sem_pvs_pe, b)
                    sp.wait_ge(sem_z_dve, UNITS_A)
                    sp.wait_ge(sem_pt_pe, PT_A)
                    sp.dma_start(vs[:, 0:4], cache_v[0, b].rearrange("(t p) k d -> p t (k d)", p=P)
                                 ).then_inc(sem_ksv_ld[0], 16)
                    sp.dma_start(vs_new, new_v_s[0, b].rearrange("t k d -> t (k d)")
                                 ).then_inc(sem_ksv_ld[0], 16)

            def stores(step):
                kind, n = step[0], NTH[step]
                if kind == "CHUNKS" or (kind == "TK" and last_rounds(step)):
                    b = step[1]
                    m = MASKS.index(b)
                    w, r = (KEYS_S, 8 * P) if b == "s" else (P * (b + 1), P * b)
                    sp.wait_ge(sem_mask, m + 1)
                    sp.dma_start(z_mask[r:r + P, 0:w], msk[:, mask_half(b), 0:w]).then_inc(sem_mask_out, 16)
                elif kind == "ZZ":
                    _, b, kv = step
                    c = block_column(b)
                    sp.wait_ge(sem_z_dve, n + 1)
                    sp.dma_start(z_mix[512 * kv:512 * kv + 512, c:c + P].rearrange("(h d) t -> d h t", d=P),
                                 zat[:].rearrange("p (h t) -> p h t", h=4)).then_inc(sem_z_out, 16)
                elif kind == "ZS":
                    sp.wait_ge(sem_vs_dve, NB)
                    sp.dma_start(z_mix[0:1024, 512:T_A].rearrange("(h d) t -> d h t", d=P), z_s
                                 ).then_inc(sem_zs_out, 16)
                elif kind == "FIN":
                    i = step[1]
                    src = fin_o[:, i % 2] if i < 5 else o_nat[:, i - 5]
                    for c in range(2):
                        cut = slice(D // 2 * c, D // 2 * (c + 1))
                        sp.wait_ge(sem_fin, 2 * n + c + 1)
                        sp.dma_start(token_rows(y_prompt[0], ys, i)[:, cut], src[:, cut]).then_inc(sem_fin_out, 16)

            def load_final(i):
                sp.wait_ge(sem_z_out, 16 * UNITS)
                sp.wait_ge(sem_z_lo, 2 * KT)
                sp.wait_ge(sem_fin, 2 * min(max(i - 1, 0), 5))
                sp.wait_ge(sem_fin_out, 32 * (max(i - 1, 0) if i < 5 else i - 3 if i > 6 else 0))
                if i < 5:
                    sp.wait_ge(sem_og_out, 16 * PAIRS)
                    sp.dma_start(fin_o[:, i % 2], z_og[P * i:P * (i + 1)]).then_inc(sem_fx_ld[final_slot(i)], 16)
                sp.dma_start(residual(i), token_rows(x_prompt[0], xs, i)).then_inc(sem_fx_ld[final_slot(i)], 16)

            load_x(0)
            sp.dma_start(gbc[:], g_pre[0:1, :].broadcast_to([P, D])).then_inc(sem_g_ld, 16)
            load_x(1)
            load_weights(0)
            load_x(2)
            load_weights(1)
            load_x(3)
            load_x(4)
            load_weights(2)
            for j in range(3):
                sp.dma_start(wcv[:, j], w_conv[0, j].rearrange("(c p) -> p c", p=P),
                             allow_slow_non_contiguous=True).then_inc(sem_wcv_ld, 16)
            for c in range(8):
                sp.dma_start(st[:, c], state_conv[0][:, :, P * c:P * (c + 1)].rearrange("b j p -> p (b j)"),
                             allow_slow_non_contiguous=True).then_inc(sem_st_ld, 16)

            for slot in range(TAIL + 1):
                n, s = divmod(slot, SLOTS)
                if n < NT and s in (0, 4):
                    load_weights(2 * n + s // 4 + RING)
                if slot:
                    for step in SIDE.get(slot - 1, ()):
                        stores(step)
                for step in LOADS.get(slot, ()):
                    index_loads(step)
                    softmax_loads(step)
                    if step[0] == "NX":
                        load_x(step[1])
                    if step[0] == "FIN":
                        load_final(step[1])
                for g in range(2):
                    if n == PHASE_LAST[1 + g]:
                        for k in range(KT):
                            if s == max(0, (k - 4 - g) // 2):
                                load_z(g, k)
                if n and s == 2 and TILES[n - 1][1] in SPILLED:
                    spill(n - 1)
                if n and s == 4 and TILES[n - 1][1] in TURNED:
                    store_turned(n - 1)
                if OUT_A < n <= OUT_B and s == 2 and TILES[n - 1][2] % 2:
                    store_product(n - 1)
                if slot == SLOTS * NP + 16:
                    sp.wait_ge(sem_x_rdy, 9)
                    sp.dma_start(gbc[:], g_post[0:1, :].broadcast_to([P, D])).then_inc(sem_g_ld, 16)
                if slot == SLOTS * (OUT_A + 2):
                    sp.wait_ge(sem_hc_rdy, 16)
                    for c in range(8):
                        part = slice(P * c, P * c + P)
                        sp.dma_start(conv_p[0, 0][:, part].rearrange("j p -> p j"), cs[:, c, 0:2],
                                     allow_slow_non_contiguous=True).then_inc(sem_cs_out, 16)
                        sp.dma_start(conv_s[0][:, :, part].rearrange("b j p -> p (b j)"), cs[:, c, 2:2 + 2 * NB],
                                     allow_slow_non_contiguous=True).then_inc(sem_cs_out, 16)
                if slot == SLOTS * (NT - 1):
                    for i in range(5, 9):
                        load_final(i)
            for step in SIDE[TAIL]:
                stores(step)
            sp.wait_ge(sem_cs_out, 16 * 16)
            sp.wait_ge(sem_fin_out, 32 * 9)
            sp.wait_ge(sem_og_out, 16 * PAIRS)
            sp.wait_ge(sem_nat_out[0], 16 * turned_before(OUT_B))
            sp.wait_ge(sem_nat_out[1], 16 * turned_before(NP))
            sp.wait_ge(sem_mask_out, 16 * len(MASKS))
            sp.wait_ge(sem_z_out, 16 * UNITS)
            sp.wait_ge(sem_zs_out, 16)
            spilled("B", "ga", 7)

        @block.gpsimd
        def _(pool):
            chain = [0]

            def link(ins):
                chain[0] += 1
                ins.then_inc(sem_pool_chain, 1)
                pool.wait_ge(sem_pool_chain, chain[0])

            def split_low(h):
                if h < 2 * NT:
                    pool.wait_ge(sem_w_hi, h + 1)
                    r = h % RING
                    nc.gpsimd.tensor_tensor(w_lo[:, r], w_raw[:, r], w_hi[:, r].bitcast(F32), ALU.subtract
                                            ).then_inc(sem_w_lo, 1)

            link(nc.gpsimd.memset(ident[:], 0.0))
            link(nc.gpsimd.affine_select(out=ident[:], in_=ident[:], compare_op=ALU.not_equal, fill=1.0, base=0,
                                         pattern=[[-1, P]], channel_multiplier=1))
            pool.sem_inc(sem_const, 1)
            link(nc.gpsimd.memset(sel[:], 0.0))
            own = sel[:, 112:112 + NS]
            for h in range(8):
                link(nc.gpsimd.affine_select(out=own, in_=own, compare_op=ALU.not_equal, fill=1.0, base=-NS * h,
                                             pattern=[[-1, NS]], channel_multiplier=1))
            pool.sem_inc(sem_const, 1)
            pool.wait_ge(sem_g_ld, 16)
            for i in range(5):
                pool.wait_ge(sem_x_sc, i + 1)
                x = xh[i % 4][1]
                nc.gpsimd.tensor_tensor(x, x, gbc[:, 1024:2048], ALU.mult).then_inc(sem_x_half, 1)
                if i in (1, 2):
                    split_low(i - 1)
            for h in range(2, 2 * NT):
                split_low(h)

        @block.tensor
        def _(pe):
            def transpose(out, in_):
                return nc.tensor.transpose(out, in_, ident[0:in_.shape[0], 0:in_.shape[0]])

            def norm_unit(m):
                i, j = UNITS_X[m]
                pe.wait_ge(sem_x_rdy, i + 1)
                if i < 5 and j == 2:
                    pe.wait_ge(sem_x_half, i + 1)
                pe.wait_ge(sem_x_lo, max(m - 3, 0))
                if m == NX_A:
                    pe.wait_ge(sem_iscs, 1)
                    pe.wait_ge(sem_isum, HEADS_A)
                    pe.wait_ge(sem_hs_r, 2 * NB)
                half = xh[i % 5 % 4 if i < 5 else i - 5][j // 2]
                for r in range(4):
                    c = P * (4 * (j % 2) + r)
                    last = transpose(ps[:, 4 + m % 4, P * r:P * r + P], half[:, c:c + P])
                last.then_inc(sem_x_tr, 1)
                if j == 3:
                    pe.wait_ge(sem_x_tr, m + 1)
                    pe.sem_inc(sem_x_read, 1)

            def gemm(n, s):
                group = TILES[n][0]
                count = 2 if group == "A" else 1
                w = TOKENS[group] // count
                bank = 2 * (n % 2)
                if s == 0:
                    pe.wait_ge(sem_evac[n % 2], n // 2)
                steps, views = range(PER * s, PER * (s + 1)), range(count)
                if n == 0:
                    steps, views = range(2 * PER * (s % 4), 2 * PER * (s % 4 + 1)), (s // 4,)
                if s % 4 == 0 or n == 0:
                    pe.wait_ge(sem_w_lo, 2 * n + steps[0] // 8 + 1)
                if n == 0:
                    pe.wait_ge(sem_x_lo, 12 if s < 4 else NX_A)
                for k in steps:
                    if n == NP and k % 4 == 0:
                        pe.wait_ge(sem_x_lo, NX_A + k + 4)
                    r = (2 * n + k // 8) % RING
                    for wt, parts in ((w_hi, (act_hi, act_lo)), (w_lo, (act_hi,))):
                        for a in parts:
                            for x in views:
                                last = nc.tensor.matmul(ps[:, bank + x, 0:w], wt[:, r, k % 8],
                                                        a[:, k, w * x:w * (x + 1)],
                                                        start=(k == 0 and wt is w_hi and a is act_hi),
                                                        stop=(k == KT - 1 and wt is w_lo))
                if s % 4 == 3 and n or n == 0 and s in (5, 7):
                    last.then_inc(sem_gemm, 1)
                elif n in PHASE_LAST[:2]:
                    last.then_inc(sem_passed, 1)

            def out_gemm(n, s):
                group, _, index, _ = TILES[n]
                tiles, pair = TT[group], index // 2 + PAIRS * (group == "B")
                quarter, h = 2 * (index % 2) + s // 4, 2 * n + s // 4
                if s % 4 == 0:
                    pe.wait_ge(sem_w_lo, h + 1)
                units = [(k, i) for j in range(0, tiles, 2) for k in range(4) for i in range(j, min(j + 2, tiles))]
                for x, (k, i) in enumerate(units[tiles * (s % 4):tiles * (s % 4 + 1)]):
                    kk = 4 * quarter + k
                    use = bank_use(pair, i)
                    if kk == 0 and i % 2 == 0:
                        if use < 4:
                            pe.wait_ge(sem_evac[use // 2], NP)
                        pe.wait_ge(sem_nat_sq, max(use - 3, 0))
                    if pair % PAIRS == 0 and i == 0:
                        pe.wait_ge(sem_z_lo, kk + 1 + KT * (group == "B"))
                    z = slice(P * i, P * (i + 1))
                    opens, closes = i % 2 == 0, i % 2 == 1 or i == tiles - 1
                    for part, (a, wt) in enumerate(((act_hi, w_hi), (act_hi, w_lo), (act_lo, w_hi))):
                        last = nc.tensor.matmul(out_place(pair, i), a[:, kk, z], out_weights(wt, h)[:, k],
                                                start=(kk == 0 and part == 0 and opens),
                                                stop=(kk == KT - 1 and part == 2 and closes))
                if s % 4 == 3:
                    last.then_inc(sem_gemm, 1)

            def turn(n):
                e, a = EV[n], 2 * (n % 2)
                pe.wait_ge(sem_ev_rdy[e % 2], e // 2 + 1)
                for i in range(TT[TILES[n][0]]):
                    last = transpose(ps[:, a + i // 4, P * (i % 4):P * (i % 4) + P], ev[:, e % 2, P * i:P * i + P])
                last.then_inc(sem_nat_pe, 1)

            def score_product(b, bank, operands):
                k, c = pieces(b)
                c = max(c, 2 * P)
                for x in range(k):
                    for i, (lhs, rhs) in enumerate(operands):
                        last = nc.tensor.matmul(ps[:, bank + x, 0:c], lhs, rhs[:, c * x:c * (x + 1)],
                                                start=(i == 0), stop=(i == len(operands) - 1))
                return last

            def index_step(step):
                kind, n = step[0], NTH[step]
                if kind == "HEAD":
                    _, b, hp = step
                    pe.wait_ge(sem_ik_lo, NTH["IK", group_of(b)] + 1)
                    pe.wait_ge(sem_qi_lo, NTH["QI", b, hp // 4] + 1)
                    if n == HEADS_A // 2:
                        pe.wait_ge(sem_z_dve, UNITS_A)
                        pe.wait_ge(sem_pt_lo, PT_A)
                        pe.wait_ge(sem_ps_cp, NB)
                        pe.wait_ge(sem_vs_dve, NB)
                    for odd in range(2):
                        pe.wait_ge(sem_isum, max(2 * n - 1 + odd, 0))
                        q = qst[:, 2 * hp + odd]
                        score_product(b, 4 + 2 * odd, ((q, keys_hi), (q, keys_lo))).then_inc(sem_head_pe, 1)
                elif kind == "IKS":
                    b = step[1]
                    pe.wait_ge(sem_iks_ld[b % 2], 16 * (b // 2 + 1))
                    pe.wait_ge(sem_isum, HEADS_A)
                    pe.wait_ge(sem_hs_r, 2 * b)
                    for t in range(4):
                        last = transpose(ps[0:ID, 4, P * t:P * t + P], iknat[:, b % 2, t])
                    last.then_inc(sem_iks_tr, 1)
                elif kind == "HS":
                    _, b, j = step
                    pe.wait_ge(sem_iks_cp, b + 1)
                    pe.wait_ge(sem_qs_ld, 16 * 25)
                    pe.wait_ge(sem_hs_r, n)
                    for x in range(2):
                        lhs = qs_v[:, b, 8 * j:8 * j + 8].rearrange("p h q -> p (h q)")
                        last = nc.tensor.matmul(ps[:, 4 + x, 0:HALF_S], lhs, ikt[:, HALF_S * x:HALF_S * (x + 1)],
                                                start=True, stop=True)
                    last.then_inc(sem_hs_pe, 1)
                elif kind == "SEL":
                    b = step[1]
                    pe.wait_ge(sem_const, 2)
                    pe.wait_ge(sem_hs_r, 2 * (b + 1))
                    for x in range(2):
                        last = nc.tensor.matmul(ps[:, 6 + x, 0:HALF_S], sel[:, 112 - NS * b:112 - NS * b + P],
                                                r_s[:, HALF_S * x:HALF_S * (x + 1)], start=(b == 0), stop=(b == NB - 1))
                    last.then_inc(sem_sel_pe, 1)

            def value_product(p, j, count):
                pe.wait_ge(sem_pt_lo, p + 1)
                for i, (lhs, rhs) in enumerate(((v_hi, pt_hi), (v_hi, pt_lo), (v_lo, pt_hi))):
                    last = nc.tensor.matmul(ps[:, 4, :], lhs[:, P * j:P * j + P], rhs[:, p % 2],
                                            start=(j == 0 and i == 0), stop=(j == count - 1 and i == 2))
                last.then_inc(sem_pv_pe, 1)

            def softmax_step(step):
                kind, n = step[0], NTH[step]
                if kind == "S":
                    _, b, kv, h = step
                    u = NTH["QQ", b, kv]
                    pe.wait_ge(sem_qq_lo, u + 1)
                    pe.wait_ge(sem_kk_lo, NTH["KK", group_of(b), kv] + 1)
                    pe.wait_ge(sem_s_max, max(n - 1, 0))
                    pe.wait_ge(sem_z_dve, u)
                    pe.wait_ge(sem_pt_lo, before(step, "PT"))
                    if n == 0:
                        pe.wait_ge(sem_x_lo, NX_A + NX_B)
                    if n == 4 * UNITS_A:
                        pe.wait_ge(sem_isum, HEADS)
                    hi, lo = q_hi[:, u % 2, P * h:P * h + P], q_lo[:, u % 2, P * h:P * h + P]
                    score_product(b, 4 + 2 * (h % 2), ((hi, keys_hi), (hi, keys_lo), (lo, keys_hi))
                                  ).then_inc(sem_s_pe, 1)
                elif kind == "PT":
                    _, b, kv, j = step
                    u = NTH["QQ", b, kv]
                    pe.wait_ge(sem_s_norm, 4 * (u + 1))
                    pe.wait_ge(sem_vv_lo, NTH["VV", group_of(b), kv] + 1)
                    pe.wait_ge(sem_pt_lo, max(n - 1, 0))
                    for h in range(4):
                        last = transpose(ps[:, 6 + n % 2, P * h:P * h + P], p_all[:, h, P * j:P * j + P])
                    last.then_inc(sem_pt_pe, 1)
                    if j > 0:
                        value_product(n - 1, j - 1, b + 1)
                elif kind == "ZZ":
                    b = step[1]
                    value_product(before(step, "PT") - 1, b, b + 1)
                elif kind == "KS":
                    b = step[1]
                    pe.wait_ge(sem_ksk_ld[b % 2], 16 * (b // 2 + 1))
                    pe.wait_ge(sem_z_dve, UNITS_A)
                    pe.wait_ge(sem_ps_cp, max(b - 1, 0))
                    for kv in range(2):
                        for t in range(4):
                            last = transpose(ps[:, 4 + kv, P * t:P * t + P], knat[:, t, P * kv:P * kv + P])
                    last.then_inc(sem_ks_tr, 1)
                elif kind == "SS":
                    b = step[1]
                    pe.wait_ge(sem_ks_cp, b + 1)
                    pe.wait_ge(sem_qqs_ld, 16 * (NB + 2))
                    pe.wait_ge(sem_vs_dve, b)
                    pe.wait_ge(sem_pt_lo, PT_A)
                    for kv in range(2):
                        for x in range(2):
                            last = nc.tensor.matmul(ps[64 * kv:64 * kv + 64, 6 + x, 0:HALF_S],
                                                    qraw[:, P * b + 64 * kv:P * b + 64 * kv + 64],
                                                    kts[:, kv, HALF_S * x:HALF_S * (x + 1)], start=True, stop=True)
                    last.then_inc(sem_ss_pe, 1)
                elif kind == "PS":
                    b = step[1]
                    pe.wait_ge(sem_ss_norm, b + 1)
                    pe.wait_ge(sem_ks_cp, min(b + 2, NB))
                    for t in range(4):
                        transpose(ps[:, 4, P * t:P * t + P], p_s[:, P * t:P * t + P])
                    transpose(ps[0:NS, 5, 0:P], p_s[:, PAST:KEYS_S]).then_inc(sem_ps_tr, 1)
                elif kind == "VS":
                    b = step[1]
                    pe.wait_ge(sem_ps_cp, b + 1)
                    pe.wait_ge(sem_ksv_ld[0], 32 * (b + 1))
                    pe.wait_ge(sem_ss_max, b + 1)
                    for kv in range(2):
                        for t in range(5):
                            r = P if t < 4 else NS
                            v = (vs[:, t] if t < 4 else vs_new)[:, P * kv:P * kv + P]
                            last = nc.tensor.matmul(ps[:, 6, 64 * kv:64 * kv + 64], v,
                                                    pts[0:r, t, 64 * kv:64 * kv + 64], start=(t == 0), stop=(t == 4))
                    last.then_inc(sem_pvs_pe, 1)

            pe.wait_ge(sem_const, 1)
            for m in range(12):
                norm_unit(m)
            for slot in range(TAIL):
                n, s = divmod(slot, SLOTS)
                if TILES[n][1] == "o":
                    out_gemm(n, s)
                else:
                    gemm(n, s)
                if slot < 4:
                    norm_unit(12 + 2 * s)
                    norm_unit(13 + 2 * s)
                if n and s == 1 and TILES[n - 1][1] in TURNED:
                    turn(n - 1)
                if n == NP - 1 and s % 2:
                    for i in range(4):
                        norm_unit(NX_A + 2 * (s - 1) + i)
                for step in SIDE.get(slot, ()):
                    index_step(step)
                    softmax_step(step)

        @block.scalar
        def _(act):
            def copy(out, in_):
                return nc.scalar.activation(out, in_, ACT.Copy)

            def split_high(h):
                if h < 2 * NT:
                    act.wait_ge(sem_w_ld[h % RING], 16 * (h // RING + 1))
                    act.wait_ge(sem_gemm, max(h - RING + 1, 0))
                    copy(w_hi[:, h % RING], w_raw[:, h % RING]).then_inc(sem_w_hi, 1)

            def squares(i):
                slot = i % 5 % 4 if i < 5 else i - 5
                act.wait_ge(sem_x_ms, max(i - 1, 0))
                act.wait_ge(sem_x_ssq, i)
                if i == 5:
                    act.wait_ge(sem_gb_used, 8)
                for c in range(2):
                    act.wait_ge(sem_x_ld[2 * slot + c], 16 * (1 + (i >= 4) + (i >= 5 and slot == 0)))
                    last = nc.scalar.activation(x_junk[c], xh[slot][c], ACT.Square, accum_out=x_sums[i % 2][:, c:c + 1])
                last.then_inc(sem_x_ssq, 1)

            def root(i):
                act.wait_ge(sem_x_ms, i + 1)
                nc.scalar.activation(x_stat[i % 2][2], x_stat[i % 2][1], ACT.Sqrt).then_inc(sem_x_rt, 1)

            def unit_high(m):
                i, j = UNITS_X[m]
                t = P * (i if i < 5 else i - 5)
                act.wait_ge(sem_x_tr, m + 1)
                if m >= NX_A:
                    passed(0, 4 * j + 3)
                copy(act_hi[:, 4 * j:4 * j + 4, t:t + P], ps[:, 4 + m % 4].rearrange("p (r t) -> p r t", r=4)
                     ).then_inc(sem_x_hi, 1)

            def passed(phase, k):
                s = k // PER
                if phase == 2:
                    act.wait_ge(sem_gemm, 2 * PHASE_LAST[2] + max(k // 4 - 1, 0))
                elif s == SLOTS - 1:
                    act.wait_ge(sem_gemm, 2 * PHASE_LAST[phase] + 2)
                elif s == 3:
                    act.wait_ge(sem_gemm, 2 * PHASE_LAST[phase] + 1)
                else:
                    act.wait_ge(sem_passed, 6 * phase + s + 1 - (s > 3))

            def z_high(g, k):
                m, t = k + KT * g, TOKENS["AB"[g]]
                passed(1 + g, k)
                place, loaded, count = z_place(g, k)
                act.wait_ge(loaded, count)
                copy(act_hi[:, k, 0:t], place).then_inc(sem_z_hi, 1)

            def evacuate(n):
                group, kind, index, _ = TILES[n]
                src, like = tile_view(n)
                c = index + 8 * (group == "B")
                act.wait_ge(sem_gemm, 2 * n + 2)
                if kind in BUFFERED and kind != "gb":
                    e = EV[n]
                    if e >= 2:
                        out, turned = ev_free(e)
                        act.wait_ge(sem_ev_out[e % 2], out)
                        act.wait_ge(sem_nat_pe, turned)
                    nc.scalar.activation(like(ev[:, e % 2]), src, ACT.Silu if kind == "ga" else ACT.Copy
                                         ).then_inc(sem_ev_rdy[e % 2], 1)
                    if kind not in TURNED:
                        act.wait_ge(sem_ev_rdy[e % 2], e // 2 + 1)
                        act.sem_inc(sem_evac[n % 2], 1)
                elif kind == "cg":
                    act.wait_ge(sem_hc_rdy, c)
                    copy(like(c_cg), src).then_inc(sem_cg_rdy, 1)
                    act.wait_ge(sem_cg_rdy, c + 1)
                    act.sem_inc(sem_evac[n % 2], 1)
                elif kind == "gb":
                    act.wait_ge(sem_gb_used, c)
                    nc.scalar.activation(like(c_g), src, ACT.Silu).then_inc(sem_gb_silu, 1)
                    act.wait_ge(sem_gb_silu, c + 1)
                    act.sem_inc(sem_evac[n % 2], 1)

            def product_squares(n):
                group, _, index, _ = TILES[n]
                pair = index // 2 + PAIRS * (group == "B")
                act.wait_ge(sem_nat_sq, bank_use(pair, 0))
                if pair == 0:
                    act.wait_ge(sem_nat_out[0], 16 * turned_before(NT))
                    act.wait_ge(sem_nat_out[1], 16 * turned_before(NP))
                if pair == PAIRS:
                    act.wait_ge(sem_o_ms, 1)
                for i in range(TT[group]):
                    act.wait_ge(sem_o_cp, bank_use(pair, i) + 1)
                    last = nc.scalar.activation(o_junk[i], out_place(pair, i), ACT.Square,
                                                accum_out=o_ssq[:, i, index // 2:index // 2 + 1])
                    if i % 2 or i == TT[group] - 1:
                        last.then_inc(sem_nat_sq, 1)

            def index_step(step):
                kind, n = step[0], NTH[step]
                if kind == "IK":
                    w = 512 if step[1] == "A" else 1024
                    act.wait_ge(sem_ik_ld, 32 if step[1] == "A" else 96)
                    if step[1] == "B":
                        act.wait_ge(sem_s_pe, 4 * UNITS_A)
                    copy(keys_hi[:, 0:w], raw[:, 0:w]).then_inc(sem_ik_hi, 1)
                elif kind == "QI":
                    act.wait_ge(sem_qi_ld, 32 * (n + 1))
                    act.wait_ge(sem_head_pe, 2 * before(step, "HEAD"))
                    if step[1] >= 4:
                        act.wait_ge(sem_pv_pe, PT_A)
                    copy(qv[:, 1024 * step[2]:1024 * step[2] + 1024], qraw[:]).then_inc(sem_qi_hi, 1)
                elif kind == "HEAD":
                    for odd in range(2):
                        act.wait_ge(sem_head_pe, 2 * n + 1 + odd)
                        v, _ = score_view(4 + 2 * odd, step[1])
                        nc.scalar.activation(v, v, ACT.Relu, scale=(ID * IH * 1.0) ** -0.5).then_inc(sem_relu, 1)
                elif kind == "IKS":
                    b = step[1]
                    act.wait_ge(sem_iks_tr, b + 1)
                    act.wait_ge(sem_hs_pe, 2 * b)
                    if b == 0:
                        act.wait_ge(sem_qs_ld, 16 * 25)
                    copy(ikt[:, PAST:KEYS_S], ik_new[:, NS * b:NS * (b + 1)])
                    copy(ikt[:, 0:PAST], ps[0:ID, 4, :]).then_inc(sem_iks_cp, 1)
                elif kind == "HS" and step[2] == 1:
                    act.wait_ge(sem_hs_pe, n + 1)
                    nc.scalar.activation(ps[:, 4:6, 0:HALF_S], ps[:, 4:6, 0:HALF_S], ACT.Relu).then_inc(sem_hs_relu, 1)

            def softmax_step(step):
                kind, n = step[0], NTH[step]
                if kind == "KK":
                    w = 512 if step[1] == "A" else 1024
                    act.wait_ge(sem_kk_ld, (16, 32, 64, 96)[n])
                    act.wait_ge(sem_s_pe, 16 * n)
                    act.wait_ge(sem_head_pe, HEADS_A if n < 2 else HEADS)
                    copy(keys_hi[:, 0:w], raw[:, 0:w]).then_inc(sem_kk_hi, 1)
                elif kind == "VV":
                    w = 512 if step[1] == "A" else 1024
                    act.wait_ge(sem_vv_ld, 16 * (n + 1))
                    act.wait_ge(sem_pv_pe, before(step, "PT"))
                    act.wait_ge(sem_head_pe, HEADS_A if n < 2 else HEADS)
                    copy(v_hi[:, 0:w], raw[:, 0:w]).then_inc(sem_vv_hi, 1)
                elif kind == "QQ":
                    u = n % 2
                    act.wait_ge(sem_qq_ld[u], 48 * (n // 2 + 1))
                    act.wait_ge(sem_s_pe, 4 * max(n - 1, 0))
                    copy(q_hi[:, u], qraw[:, 512 * u:512 * u + 512]).then_inc(sem_qq_hi, 1)
                elif kind == "S":
                    _, b, kv, h = step
                    act.wait_ge(sem_s_nb, n + 1)
                    p = p_all[:, h, 0:P * (b + 1)]
                    nc.scalar.activation(p, p, ACT.Exp, bias=nb_[:, h:h + 1], scale=SCALE, accum_out=sm[:, h:h + 1]
                                         ).then_inc(sem_s_exp, 1)
                elif kind == "PT":
                    act.wait_ge(sem_pt_pe, n + 1)
                    act.wait_ge(sem_pv_pe, max(n - 1, 0))
                    copy(pt_hi[:, n % 2], ps[:, 6 + n % 2]).then_inc(sem_pt_hi, 1)
                elif kind == "KS":
                    b = step[1]
                    act.wait_ge(sem_ks_tr, b + 1)
                    act.wait_ge(sem_pt_pe, PT_A)
                    act.wait_ge(sem_ss_pe, b)
                    if b == 0:
                        act.wait_ge(sem_qqs_ld, 16 * (NB + 2))
                    copy(kts[:, :, PAST:KEYS_S], k_new[:, :, NS * b:NS * (b + 1)])
                    copy(kts[:, :, 0:PAST], ps[:, 4:6]).then_inc(sem_ks_cp, 1)
                elif kind == "SS":
                    act.wait_ge(sem_ss_nb, n + 1)
                    nc.scalar.activation(p_s, p_s, ACT.Exp, bias=nb_s, scale=SCALE, accum_out=sm_s
                                         ).then_inc(sem_ss_exp, 1)
                elif kind == "PS":
                    act.wait_ge(sem_ps_tr, n + 1)
                    act.wait_ge(sem_pvs_pe, n)
                    copy(pts[:, 0:4], ps[:, 4].rearrange("p (t n) -> p t n", t=4))
                    copy(pts[0:NS, 4], ps[0:NS, 5, 0:P]).then_inc(sem_ps_cp, 1)

            def root_step(step):
                if step[0] == "RMS":
                    n = NTH[step]
                    act.wait_ge(sem_o_ms, n + 1)
                    nc.scalar.activation(o_stat[2], o_stat[1], ACT.Sqrt).then_inc(sem_o_rt, 1)

            def divide_x(i):
                act.wait_ge(sem_x_rs, i + 1)
                x = xh[i % 4][1]
                nc.scalar.activation(x, x, ACT.Copy, scale=x_stat[i % 2][3]).then_inc(sem_x_sc, 1)

            act.wait_ge(sem_const, 1)
            nc.scalar.activation(stat[:, 63:64], ident[:, 0:1], ACT.Sqrt)
            squares(0)
            root(0)
            divide_x(0)
            squares(1)
            root(1)
            divide_x(1)
            squares(2)
            for m in range(0, 4):
                unit_high(m)
            split_high(0)
            root(2)
            divide_x(2)
            for m in range(4, 8):
                unit_high(m)
            squares(3)
            for m in range(8, 12):
                unit_high(m)
            split_high(1)
            root(3)
            divide_x(3)
            squares(4)
            for m in range(12, 16):
                unit_high(m)
            root(4)
            divide_x(4)
            for m in range(16, 20):
                unit_high(m)
            for slot in range(TAIL + SLOTS):
                n, s = divmod(slot, SLOTS)
                if n and s == 0:
                    evacuate(n - 1)
                if n < NT and s in (0, 4):
                    split_high(2 * n + s // 4 + RING - 1)
                if n and s == 0 and TILES[n - 1][1] == "o" and TILES[n - 1][2] % 2:
                    product_squares(n - 1)
                if n == NP - 1 and s % 2:
                    for i in range(4):
                        unit_high(NX_A + 2 * (s - 1) + i)
                if slot < TAIL:
                    for step in SIDE.get(slot, ()):
                        index_step(step)
                        softmax_step(step)
                        root_step(step)
                        if step[0] == "NX":
                            squares(step[1])
                            root(step[1])
                for g, k in z_pieces(slot):
                    z_high(g, k)
            root_step(("RMS", "B"))

        @block.vector
        def _(dve):
            chain = [0]

            def link(ins):
                chain[0] += 1
                ins.then_inc(sem_dve_chain, 1)
                dve.wait_ge(sem_dve_chain, chain[0])

            def low(out, x, hi):
                return nc.vector.tensor_tensor(out, x, hi.bitcast(F32), ALU.subtract)

            def inverse_root(s):
                link(nc.vector.reciprocal(s[3], s[2]))
                link(nc.vector.tensor_tensor(s[2], s[3], s[3], ALU.mult))
                link(nc.vector.tensor_tensor(s[2], s[2], s[1], ALU.mult))
                link(nc.vector.tensor_scalar(s[2], s[2], -0.5, 1.5, ALU.mult, ALU.add))
                return nc.vector.tensor_tensor(s[3], s[3], s[2], ALU.mult)

            def mean_square(i):
                dve.wait_ge(sem_x_ssq, i + 1)
                x, sums = x_stat[i % 2], x_sums[i % 2]
                link(nc.vector.tensor_tensor(x[0], sums[:, 0:1], sums[:, 1:2], ALU.add))
                nc.vector.tensor_scalar(x[1], x[0], 1.0 / D, EPS, ALU.mult, ALU.add).then_inc(sem_x_ms, 1)

            def normalise_x(i):
                slot = i % 5 % 4 if i < 5 else i - 5
                dve.wait_ge(sem_x_rt, i + 1)
                dve.wait_ge(sem_x_sc, min(max(i - 1, 0), 5))
                inverse_root(x_stat[i % 2]).then_inc(sem_x_rs, 1)
                dve.wait_ge(sem_x_rs, i + 1)
                if i == 0:
                    dve.wait_ge(sem_g_ld, 16)
                for c in range(1 if i < 5 else 2):
                    x = xh[slot][c]
                    last = nc.vector.scalar_tensor_tensor(out=x, in0=x, scalar=x_stat[i % 2][3],
                                                          in1=gbc[:, 1024 * c:1024 * (c + 1)],
                                                          op0=ALU.mult, op1=ALU.mult)
                last.then_inc(sem_x_rdy, 1)

            def unit_low(m):
                i, j = UNITS_X[m]
                t = P * (i if i < 5 else i - 5)
                dve.wait_ge(sem_x_hi, m + 1)
                cut = (slice(None), slice(4 * j, 4 * j + 4), slice(t, t + P))
                low(act_lo[cut], ps[:, 4 + m % 4].rearrange("p (r t) -> p r t", r=4), act_hi[cut]).then_inc(sem_x_lo, 1)

            def z_low(g, k):
                m, t = k + KT * g, TOKENS["AB"[g]]
                dve.wait_ge(sem_z_hi, m + 1)
                low(act_lo[:, k, 0:t], z_place(g, k)[0], act_hi[:, k, 0:t]).then_inc(sem_z_lo, 1)

            def conv_input(n):
                group, _, c, _ = TILES[n]
                m, a = c + 8 * (group == "B"), 2 * (n % 2)
                if m == 0:
                    dve.wait_ge(sem_wcv_ld, 16 * 3)
                    dve.wait_ge(sem_st_ld, 16 * 8)
                dve.wait_ge(sem_gemm, 2 * n + 2)
                dve.wait_ge(sem_cg_rdy, m + 1)
                if group == "A":
                    nc.vector.memset(c_up[:, 0:2], 0.0)
                    nc.vector.tensor_copy(c_us[:, :, 0:2], st[:, c].rearrange("p (b j) -> p b j", b=NB))
                    nc.vector.tensor_tensor(c_up[:, 2:322], ps[:, a, 0:320], c_cg[:, 0:320], ALU.mult)
                    nc.vector.tensor_tensor(c_up[:, 322:514], ps[:, a + 1, 0:192], c_cg[:, 320:512], ALU.mult)
                    link(nc.vector.tensor_tensor(c_us[:, :, 2:18],
                                                 ps[:, a + 1, 192:320].rearrange("p (b t) -> p b t", b=NB),
                                                 c_cg[:, 512:640].rearrange("p (b t) -> p b t", b=NB), ALU.mult))
                    nc.vector.tensor_copy(cs[:, c, 2:18].rearrange("p (b j) -> p b j", b=NB), c_us[:, :, 16:18])
                    nc.vector.tensor_copy(u_prev[:, c], c_up[:, 512:514]).then_inc(sem_hc_rdy, 1)
                else:
                    nc.vector.tensor_copy(c_up[:, 0:2], u_prev[:, c])
                    link(nc.vector.tensor_tensor(c_up[:, 2:514], ps[:, a, 0:512], c_cg[:, 0:512], ALU.mult))
                    nc.vector.tensor_copy(cs[:, c, 0:2], c_up[:, 512:514]).then_inc(sem_hc_rdy, 1)
                dve.wait_ge(sem_hc_rdy, m + 1)
                dve.sem_inc(sem_evac[n % 2], 1)

            def conv_taps(n):
                group, _, c, _ = TILES[n]
                yp, ys_ = c_y[:, 0:512], c_y[:, 512:640].rearrange("p (b t) -> p b t", b=NB)
                parts = [(yp, lambda j: c_up[:, j:j + 512])]
                if group == "A":
                    parts.append((ys_, lambda j: c_us[:, :, j:j + NS]))
                for j in range(3):
                    w = wcv[:, j, c:c + 1]
                    for x, (y, u) in enumerate(parts):
                        if j == 0:
                            ins = nc.vector.tensor_scalar(y, u(0), w, None, ALU.mult)
                        else:
                            ins = nc.vector.scalar_tensor_tensor(out=y, in0=u(j), scalar=w, in1=y, op0=ALU.mult,
                                                                 op1=ALU.add)
                        if x == len(parts) - 1:
                            link(ins)
                src, like = tile_view(n)
                dve.wait_ge(sem_gemm, 2 * n + 2)
                link(nc.vector.tensor_tensor(like(c_y), src, like(c_y), ALU.mult))
                dve.sem_inc(sem_evac[n % 2], 1)

            def conv_gate(n):
                group, _, c, _ = TILES[n]
                t, e = TOKENS[group], EV[n]
                dve.wait_ge(sem_gb_silu, c + 8 * (group == "B") + 1)
                out, turned = ev_free(e)
                dve.wait_ge(sem_ev_out[e % 2], out)
                dve.wait_ge(sem_nat_pe, turned)
                nc.vector.tensor_tensor(ev[:, e % 2, 0:t], c_y[:, 0:t], c_g[:, 0:t], ALU.mult
                                        ).then_inc(sem_ev_rdy[e % 2], 1)
                dve.wait_ge(sem_ev_rdy[e % 2], e // 2 + 1)
                dve.sem_inc(sem_gb_used, 1)

            def turned_out(n):
                group, kind, index, _ = TILES[n]
                m, a, k = TURN[n], 2 * (n % 2), TT[TILES[n][0]]
                dve.wait_ge(sem_nat_pe, m + 1)
                first = ps[:, a].rearrange("p (i d) -> p i d", i=4)
                dve.wait_ge(sem_nat_out[0], 16 * m)
                dve.wait_ge(sem_nat_out[1], 16 * turned_before(n, "A"))
                if k == 5:
                    nc.vector.tensor_copy(nat[:, 4], ps[:, a + 1, 0:P])
                link(nc.vector.tensor_copy(nat[:, 0:4], first))
                if kind == "kiwi":
                    w0 = 0 if group == "A" else 5
                    link(nc.vector.tensor_copy(wi_nat[:, w0:w0 + k], nat[:, 0:k, ID:ID + IH]))
                dve.sem_inc(sem_nat_cp, 1)
                dve.sem_inc(sem_evac[n % 2], 1)

            def product_out(n):
                group, _, index, c = TILES[n]
                pair = index // 2 + PAIRS * (group == "B")
                dve.wait_ge(sem_gemm, 2 * n + 2)
                if pair == 0:
                    dve.wait_ge(sem_g_ld, 32)
                    dve.wait_ge(sem_ev_out[0], 16 * EV_SPILLS[max(EV)][0])
                    dve.wait_ge(sem_ev_out[1], 16 * EV_SPILLS[max(EV)][1])
                    dve.wait_ge(sem_nat_pe, len(TURN))
                if group == "A":
                    dve.wait_ge(sem_og_out, 16 * pair)
                if pair == PAIRS:
                    dve.wait_ge(sem_z_out, 16 * UNITS)
                for i in range(TT[group]):
                    out = o_stage[:, i] if group == "A" else o_nat[:, i, c:c + OW]
                    last = nc.vector.tensor_tensor(out, out_place(pair, i), gbc[:, c:c + OW], ALU.mult)
                    if i % 2 or i == TT[group] - 1:
                        last.then_inc(sem_o_cp, 1)

            def index_step(step):
                kind, n = step[0], NTH[step]
                if kind == "IK":
                    w = 512 if step[1] == "A" else 1024
                    dve.wait_ge(sem_ik_hi, n + 1)
                    low(keys_lo[:, 0:w], raw[:, 0:w], keys_hi[:, 0:w]).then_inc(sem_ik_lo, 1)
                elif kind == "QI":
                    dve.wait_ge(sem_qi_hi, n + 1)
                    cut = (slice(64, 128), slice(1024 * step[2], 1024 * step[2] + 1024))
                    low(qv[cut], qraw[64:128, :], qv[cut]).then_inc(sem_qi_lo, 1)
                elif kind == "HEAD":
                    _, b, hp = step
                    t = b + (b >= 4)
                    for odd in range(2):
                        dve.wait_ge(sem_relu, 2 * n + 1 + odd)
                        v, like = score_view(4 + 2 * odd, b)
                        wi = wi_nat[:, t, 2 * hp + odd:2 * hp + odd + 1]
                        if hp == 0 and odd == 0:
                            if n:
                                dve.wait_ge(sem_pvs_pe, NB if b >= 4 else 0)
                            ins = nc.vector.tensor_scalar(like(isc), v, wi, None, ALU.mult)
                        else:
                            dve.wait_ge(sem_isum, 2 * n + odd)
                            ins = nc.vector.scalar_tensor_tensor(out=like(isc), in0=v, scalar=wi, in1=like(isc),
                                                                 op0=ALU.mult, op1=ALU.add)
                        ins.then_inc(sem_isum, 1)
                elif kind == "TK":
                    _, b, r0 = step
                    w = KEYS_S + PAD_S if b == "s" else P * (b + 1)
                    if r0 == 0 and b == "s":
                        dve.wait_ge(sem_iscs, 1)
                    if r0 == 0 and b != "s":
                        dve.wait_ge(sem_isum, 2 * before(step, "HEAD"))
                        link(nc.vector.memset(isc[0:64, w - 64:w], NEG_LATER))
                    for r in range(r0, min(r0 + 2, ROUNDS_S if b == "s" else ROUNDS)):
                        link(nc.vector.max(top8[:], isc[:, 0:w]))
                        link(nc.vector.match_replace(isc[:, 0:w], top8[:], isc[:, 0:w], NEG_TAKEN))
                    if last_rounds(step):
                        dve.wait_ge(sem_mask_out, 16 * MASKS.index(b))
                        w = KEYS_S if b == "s" else w
                        link(nc.vector.tensor_scalar(msk[:, mask_half(b), 0:w], isc[:, 0:w], NEG_CUT, NEG_MASK,
                                                     ALU.is_gt, ALU.mult))
                        dve.sem_inc(sem_mask, 1)
                elif kind == "CHUNKS":
                    w = P * (step[1] + 1)
                    dve.wait_ge(sem_mask_out, 16 * MASKS.index(step[1]))
                    link(nc.vector.memset(msk[:, 0, 0:w], 0.0))
                    link(nc.vector.memset(msk[0:64, 0, w - 64:w], NEG_MASK))
                    dve.sem_inc(sem_mask, 1)
                elif kind == "HS":
                    _, b, j = step
                    out, v, wi = r_s.rearrange("p (a n) -> p a n", a=2), ps[:, 4:6, 0:HALF_S], wicol[:, j, b:b + 1]
                    if j == 0:
                        dve.wait_ge(sem_hs_pe, n + 1)
                        dve.wait_ge(sem_sel_pe, b)
                        nc.vector.tensor_scalar(out, v, 0.0, wi, ALU.max, ALU.mult).then_inc(sem_hs_r, 1)
                    else:
                        dve.wait_ge(sem_hs_relu, b + 1)
                        dve.wait_ge(sem_hs_r, n)
                        nc.vector.scalar_tensor_tensor(out=out, in0=v, scalar=wi, in1=out, op0=ALU.mult, op1=ALU.add
                                                       ).then_inc(sem_hs_r, 1)
                elif kind == "ISCS":
                    dve.wait_ge(sem_sel_pe, NB)
                    nc.vector.memset(isc[:, KEYS_S:KEYS_S + PAD_S], 3.0e38)
                    nc.vector.tensor_copy(isc[:, 0:KEYS_S].rearrange("p (a n) -> p a n", a=2), ps[:, 6:8, 0:HALF_S]
                                          ).then_inc(sem_iscs, 1)

            def divide(b, h, n):
                dve.wait_ge(sem_s_exp, n + 1)
                link(nc.vector.reciprocal(rs[:, h:h + 1], sm[:, h:h + 1]))
                p = p_all[:, h, 0:P * (b + 1)]
                nc.vector.tensor_scalar(p, p, rs[:, h:h + 1], None, ALU.mult).then_inc(sem_s_norm, 1)

            def softmax_step(step):
                kind, n = step[0], NTH[step]
                if kind == "KK":
                    w = 512 if step[1] == "A" else 1024
                    dve.wait_ge(sem_kk_hi, n + 1)
                    low(keys_lo[:, 0:w], raw[:, 0:w], keys_hi[:, 0:w]).then_inc(sem_kk_lo, 1)
                elif kind == "VV":
                    w = 512 if step[1] == "A" else 1024
                    dve.wait_ge(sem_vv_hi, n + 1)
                    low(v_lo[:, 0:w], raw[:, 0:w], v_hi[:, 0:w]).then_inc(sem_vv_lo, 1)
                elif kind == "QQ":
                    u = n % 2
                    dve.wait_ge(sem_qq_hi, n + 1)
                    low(q_lo[:, u], qraw[:, 512 * u:512 * u + 512], q_hi[:, u]).then_inc(sem_qq_lo, 1)
                elif kind == "S":
                    _, b, kv, h = step
                    dve.wait_ge(sem_s_pe, n + 1)
                    if h == 0:
                        dve.wait_ge(sem_pt_pe, before(step, "PT"))
                        dve.wait_ge(sem_x_read, 9)
                        dve.wait_ge(sem_pvs_pe, before(step, "VS"))
                    v, like = score_view(4 + 2 * (h % 2), b)
                    nc.vector.tensor_tensor_reduce(out=like(p_all[:, h]), in0=v, in1=like(msk[:, NTH["QQ", b, kv] % 2]),
                                                   scale=1.0, scalar=-3.0e38, op0=ALU.add, op1=ALU.max,
                                                   accum_out=mx[:, h:h + 1]).then_inc(sem_s_max, 1)
                    dve.wait_ge(sem_s_max, n + 1)
                    nc.vector.tensor_scalar(nb_[:, h:h + 1], mx[:, h:h + 1], -SCALE, None, ALU.mult
                                            ).then_inc(sem_s_nb, 1)
                    if h > 0:
                        divide(b, h - 1, n - 1)
                elif kind == "NRM":
                    _, b, kv = step
                    divide(b, 3, NTH["S", b, kv, 3])
                elif kind == "PT":
                    dve.wait_ge(sem_pt_hi, n + 1)
                    low(pt_lo[:, n % 2], ps[:, 6 + n % 2], pt_hi[:, n % 2]).then_inc(sem_pt_lo, 1)
                elif kind == "ZZ":
                    dve.wait_ge(sem_pv_pe, before(step, "PT"))
                    dve.wait_ge(sem_z_out, 16 * n)
                    nc.vector.tensor_tensor(zat[:], ps[:, 4], sga[:, n % 2], ALU.mult).then_inc(sem_z_dve, 1)
                elif kind == "SS":
                    b = step[1]
                    dve.wait_ge(sem_ss_pe, b + 1)
                    dve.wait_ge(sem_ksm_ld[b % 2], 16 * 8 * (b // 2 + 1))
                    dve.wait_ge(sem_ps_tr, b)
                    dve.wait_ge(sem_pt_pe, PT_A)
                    m = msk[:, b % 2, 0:KEYS_S].rearrange("p (a n) -> p a n", a=2)
                    nc.vector.tensor_tensor_reduce(out=p_s.rearrange("p (a n) -> p a n", a=2), in0=ps[:, 6:8, 0:HALF_S],
                                                   in1=m, scale=1.0, scalar=-3.0e38, op0=ALU.add, op1=ALU.max,
                                                   accum_out=mx_s).then_inc(sem_ss_max, 1)
                    dve.wait_ge(sem_ss_max, n + 1)
                    nc.vector.tensor_scalar(nb_s, mx_s, -SCALE, None, ALU.mult).then_inc(sem_ss_nb, 1)
                    dve.wait_ge(sem_ss_exp, n + 1)
                    link(nc.vector.reciprocal(rs_s, sm_s))
                    nc.vector.tensor_scalar(p_s, p_s, rs_s, None, ALU.mult).then_inc(sem_ss_norm, 1)
                elif kind == "VS":
                    b = step[1]
                    dve.wait_ge(sem_pvs_pe, b + 1)
                    g = z_s[:, :, NS * b:NS * b + NS]
                    nc.vector.tensor_tensor(g, ps[:, 6, 0:P].rearrange("p (h q) -> p h q", h=8), g, ALU.mult
                                            ).then_inc(sem_vs_dve, 1)

            def final_step(step):
                kind, n = step[0], NTH[step]
                if kind == "RMS":
                    k = TT[step[1]]
                    dve.wait_ge(sem_nat_sq, bank_use(PAIRS * (n + 1), 0))
                    dve.wait_ge(sem_fin, 10 * n)
                    link(nc.vector.tensor_reduce(o_stat[0][:, 0:k], o_ssq[:, 0:k, :], AX_X, ALU.add))
                    nc.vector.tensor_scalar(o_stat[1], o_stat[0], 1.0 / D, EPS, ALU.mult, ALU.add).then_inc(sem_o_ms, 1)
                    dve.wait_ge(sem_o_rt, n + 1)
                    link(inverse_root(o_stat))
                elif kind == "FIN":
                    i = step[1]
                    dve.wait_ge(sem_fx_ld[final_slot(i)], FIN_LOADS[i])
                    o, r = (fin_o[:, i % 2], i) if i < 5 else (o_nat[:, i - 5], i - 5)
                    for c in range(2):
                        cut = slice(D // 2 * c, D // 2 * (c + 1))
                        nc.vector.scalar_tensor_tensor(out=o[:, cut], in0=o[:, cut], scalar=o_stat[3][:, r:r + 1],
                                                       in1=residual(i)[:, cut], op0=ALU.mult, op1=ALU.add
                                                       ).then_inc(sem_fin, 1)

            nc.vector.memset(o_stat[0], 0.0)
            mean_square(0)
            normalise_x(0)
            mean_square(1)
            normalise_x(1)
            mean_square(2)
            for m in range(0, 4):
                unit_low(m)
            normalise_x(2)
            for m in range(4, 8):
                unit_low(m)
            mean_square(3)
            for m in range(8, 12):
                unit_low(m)
            normalise_x(3)
            mean_square(4)
            for m in range(12, 16):
                unit_low(m)
            normalise_x(4)
            for m in range(16, 20):
                unit_low(m)
            for slot in range(TAIL + SLOTS):
                n, s = divmod(slot, SLOTS)
                if n and s == 0 and TILES[n - 1][1] == "hc":
                    conv_input(n - 1)
                if n and s == 0 and TILES[n - 1][1] == "bg":
                    conv_taps(n - 1)
                if n and s == 1 and TILES[n - 1][1] == "gb":
                    conv_gate(n - 1)
                if n and s == 2 and TILES[n - 1][1] in TURNED:
                    turned_out(n - 1)
                if n and s == 0 and TILES[n - 1][1] == "o" and TILES[n - 1][2] % 2:
                    product_out(n - 1)
                if n == NP - 1 and s % 2:
                    for i in range(4):
                        unit_low(NX_A + 2 * (s - 1) + i)
                if slot < TAIL:
                    for step in SIDE.get(slot, ()):
                        index_step(step)
                        softmax_step(step)
                        final_step(step)
                        if step[0] == "NX":
                            mean_square(step[1])
                            normalise_x(step[1])
                for g, k in z_pieces(slot):
                    z_low(g, k)
            for step in SIDE[TAIL]:
                final_step(step)


FIN_LOADS = [32 * (i // 2 + 1) if i < 5 else 16 for i in range(9)]


def final_slot(i):
    return i % 2 if i < 5 else i - 3


_INS = ["x_prompt", "x_sample", "cache_k", "cache_v", "cache_idx_k", "state_conv", "g_pre", "w_in", "w_conv",
        "w_out", "g_post"]
_OUTS = [(1, 1024, 2048), (8, 16, 2048), (1, 1, 1024, 2, 128), (1, 1, 1024, 2, 128), (1, 1, 1024, 64),
         (1, 1, 2, 1024), (1, 8, 16, 2, 128), (1, 8, 16, 2, 128), (1, 8, 16, 64), (1, 8, 2, 1024)]


def kernel(**inputs):
    import numpy as np
    import concourse.bacc as bacc
    from concourse.bass_utils import run_bass_kernel_spmd

    nc = bacc.Bacc("TRN2", target_bir_lowering=False, num_devices=1, dynamic_dma_scratch_size=1024)
    arrays, args = {}, []
    for name in _INS:
        a = np.ascontiguousarray(inputs[name])
        arrays["in_" + name] = a
        args.append(nc.dram_tensor("in_" + name, a.shape, mybir.dt.from_np(a.dtype), kind="ExternalInput").ap())
    for i, shape in enumerate(_OUTS):
        args.append(nc.dram_tensor(f"out_{i}", shape, F32, kind="ExternalOutput").ap())
    build(nc, *args)
    r = run_bass_kernel_spmd(nc, [arrays], core_ids=[0])
    return tuple(r.results[0][f"out_{i}"] for i in range(len(_OUTS)))
```
